# Optimizing a Trainium2 kernel written in Bass

```python
import math
import jax, jax.numpy as jnp
from jax import lax
import numpy as np

D_MODEL = 1024
BATCH = 1
SEQ = 256
DEPTH = 1

CHUNK = 64
N_PREV_CHUNKS = 8
HEAD_DIM = 64
N_HEADS_A = 8
REL_CLIP = 128
N_HEADS_B = 8
N_KV_B = 2
N_IDX_HEADS = 8
IDX_DIM = 64
TOPK_MAX = 256
Q_BLOCK = 128
ROPE_THETA = 500000.0
ROT_DIM = HEAD_DIM // 4
D_FF = 2816
EPS = 1e-6

WIDTH_A = N_HEADS_A * HEAD_DIM
WIDTH_B = N_HEADS_B * HEAD_DIM
WIDTH_KV_B = N_KV_B * HEAD_DIM
SPLIT_SIZES = (WIDTH_A, WIDTH_A, WIDTH_A,
               WIDTH_B, WIDTH_KV_B, WIDTH_KV_B,
               N_IDX_HEADS * IDX_DIM, IDX_DIM,
               N_IDX_HEADS,
               D_MODEL, D_MODEL)
D_IN = sum(SPLIT_SIZES)


def _rmsnorm(x, g):
    xf = x.astype(jnp.float32)
    y = xf * lax.rsqrt(jnp.mean(xf * xf, axis=-1, keepdims=True) + EPS)
    return (y * g.astype(jnp.float32)).astype(x.dtype)

def _swiglu(x, w_in, w_out):
    gate, up = jnp.split(x @ w_in, 2, axis=-1)
    return (jax.nn.silu(gate) * up) @ w_out

def _rope_tables(seq):
    inv_freq = jnp.power(jnp.float32(ROPE_THETA), -jnp.arange(0, ROT_DIM, 2, dtype=jnp.float32) / ROT_DIM)
    ang = jnp.arange(seq, dtype=jnp.float32)[:, None] * inv_freq[None, :]
    return jnp.cos(ang)[:, None, :], jnp.sin(ang)[:, None, :]

def _partial_rope(t, cos, sin):
    tr = t[..., :ROT_DIM].astype(jnp.float32)
    t1, t2 = tr[..., :ROT_DIM // 2], tr[..., ROT_DIM // 2:]
    rot = jnp.concatenate([t1 * cos - t2 * sin, t2 * cos + t1 * sin], axis=-1)
    return jnp.concatenate([rot.astype(t.dtype), t[..., ROT_DIM:]], axis=-1)

def _mixer_a(q, k, v, rel_bias):
    B, S, H, Dh = q.shape
    nc = S // CHUNK
    band_len = (N_PREV_CHUNKS + 1) * CHUNK
    qc = q.reshape(B, nc, CHUNK, H, Dh)

    def band(t):
        tp = jnp.pad(t, ((0, 0), (N_PREV_CHUNKS * CHUNK, 0), (0, 0), (0, 0)))
        tp = tp.reshape(B, nc + N_PREV_CHUNKS, CHUNK, H, Dh)
        return jnp.concatenate([tp[:, j:j + nc] for j in range(N_PREV_CHUNKS + 1)], axis=2)

    kb, vb = band(k), band(v)
    s = jnp.einsum('bnqhd,bnkhd->bnhqk', qc, kb).astype(jnp.float32) * (Dh ** -0.5)
    qi = jnp.arange(CHUNK)
    kj = jnp.arange(band_len)
    dist = N_PREV_CHUNKS * CHUNK + qi[:, None] - kj[None, :]
    bias = rel_bias[:, jnp.clip(dist, -REL_CLIP, REL_CLIP) + REL_CLIP].astype(jnp.float32)
    key_pos = (jnp.arange(nc)[:, None] - N_PREV_CHUNKS) * CHUNK + kj[None, :]
    valid = (key_pos >= 0)[None, :, None, None, :]
    s = jnp.where(valid, s + bias[None, None], -jnp.inf)
    p = jax.nn.softmax(s, axis=-1).astype(vb.dtype)
    o = jnp.einsum('bnhqk,bnkhd->bnqhd', p, vb)
    return o.reshape(B, S, H * Dh)

def _to_blocks(a):
    B, S = a.shape[:2]
    return jnp.moveaxis(a.reshape((B, S // Q_BLOCK, Q_BLOCK) + a.shape[2:]), 1, 0)

def _mixer_b(q, k, v, q_idx, k_idx, w_idx):
    B, S, H, Dh = q.shape
    G = k.shape[2]
    R = H // G
    topk = min(TOPK_MAX, S // 4)
    nb = S // Q_BLOCK
    key_pos = jnp.arange(S)
    w_scaled = w_idx * (N_IDX_HEADS ** -0.5)

    def one_block(args):
        qb, qib, wb, pos_q = args
        sc = jnp.einsum('bqhd,bsd->bqhs', qib, k_idx).astype(jnp.float32) * (IDX_DIM ** -0.5)
        score = jnp.einsum('bqh,bqhs->bqs', wb.astype(jnp.float32), jax.nn.relu(sc))
        limit = (pos_q // CHUNK + 1) * CHUNK
        adm = key_pos[None, :] < limit[:, None]
        score = jnp.where(adm[None], score, -jnp.inf)
        _, idx = lax.top_k(score, topk)
        sel_ok = idx < limit[None, :, None]
        kg = jax.vmap(lambda t, i: t[i])(k, idx)
        vg = jax.vmap(lambda t, i: t[i])(v, idx)
        qg = qb.reshape(B, Q_BLOCK, G, R, Dh)
        s = jnp.einsum('bqgrd,bqkgd->bqgrk', qg, kg).astype(jnp.float32) * (Dh ** -0.5)
        s = jnp.where(sel_ok[:, :, None, None, :], s, -jnp.inf)
        p = jax.nn.softmax(s, axis=-1).astype(vg.dtype)
        o = jnp.einsum('bqgrk,bqkgd->bqgrd', p, vg)
        return o.reshape(B, Q_BLOCK, H * Dh)

    out = lax.map(one_block, (_to_blocks(q), _to_blocks(q_idx), _to_blocks(w_scaled),
                              key_pos.reshape(nb, Q_BLOCK)))
    return jnp.moveaxis(out, 0, 1).reshape(B, S, H * Dh)

def first_inputs(seed: int = 0) -> dict:
    key = jax.random.key(seed)
    ks = jax.random.split(key, 16)
    f32 = jnp.float32

    def w(k, shape, fan_in):
        return jax.random.normal(k, shape, f32) * (fan_in ** -0.5)

    def gain(k):
        return 1.0 + 0.02 * jax.random.normal(k, (DEPTH, D_MODEL), f32)

    return {
        'x': jax.random.normal(ks[0], (BATCH, SEQ, D_MODEL), f32),
        'n1_g': gain(ks[1]),
        'ffn1_w_in': w(ks[2], (DEPTH, D_MODEL, 2 * D_FF), D_MODEL),
        'ffn1_w_out': w(ks[3], (DEPTH, D_FF, D_MODEL), D_FF),
        'n2_g': gain(ks[4]),
        'w_in': w(ks[5], (DEPTH, D_MODEL, D_IN), D_MODEL),
        'rel_bias': 0.2 * jax.random.normal(ks[6], (DEPTH, N_HEADS_A, 2 * REL_CLIP + 1), f32),
        'w_branch_a': w(ks[7], (DEPTH, WIDTH_A, D_MODEL), WIDTH_A),
        'w_branch_b': w(ks[8], (DEPTH, WIDTH_B, D_MODEL), WIDTH_B),
        'w_out': w(ks[9], (DEPTH, D_MODEL, D_MODEL), D_MODEL),
        'n3_g': gain(ks[10]),
        'ffn2_w_in': w(ks[11], (DEPTH, D_MODEL, 2 * D_FF), D_MODEL),
        'ffn2_w_out': w(ks[12], (DEPTH, D_FF, D_MODEL), D_FF),
        'nf_g': 1.0 + 0.02 * jax.random.normal(ks[13], (D_MODEL,), f32),
    }

def first_block(x, n1_g, ffn1_w_in, ffn1_w_out, n2_g, w_in, rel_bias, w_branch_a, w_branch_b,
              w_out, n3_g, ffn2_w_in, ffn2_w_out, nf_g):
    B, S, _ = x.shape
    cos, sin = _rope_tables(S)
    split_points = list(np.cumsum(SPLIT_SIZES)[:-1])
    for l in range(DEPTH):
        x = x + 0.5 * _swiglu(_rmsnorm(x, n1_g[l]), ffn1_w_in[l], ffn1_w_out[l])
        h = _rmsnorm(x, n2_g[l])
        qa, ka, va, qb, kb, vb, qi, ki, wi, ga, gb = jnp.split(h @ w_in[l], split_points, axis=-1)
        qa = qa.reshape(B, S, N_HEADS_A, HEAD_DIM)
        ka = ka.reshape(B, S, N_HEADS_A, HEAD_DIM)
        va = va.reshape(B, S, N_HEADS_A, HEAD_DIM)
        qb = _partial_rope(qb.reshape(B, S, N_HEADS_B, HEAD_DIM), cos, sin)
        kb = _partial_rope(kb.reshape(B, S, N_KV_B, HEAD_DIM), cos, sin)
        vb = vb.reshape(B, S, N_KV_B, HEAD_DIM)
        qi = _partial_rope(qi.reshape(B, S, N_IDX_HEADS, IDX_DIM), cos, sin)
        ki = _partial_rope(ki.reshape(B, S, 1, IDX_DIM), cos, sin)[:, :, 0]
        o_a = _mixer_a(qa, ka, va, rel_bias[l])
        o_b = _mixer_b(qb, kb, vb, qi, ki, wi)
        merged = jax.nn.sigmoid(ga) * (o_a @ w_branch_a[l]) + jax.nn.sigmoid(gb) * (o_b @ w_branch_b[l])
        x = x + merged @ w_out[l]
        x = x + 0.5 * _swiglu(_rmsnorm(x, n3_g[l]), ffn2_w_in[l], ffn2_w_out[l])
    return _rmsnorm(x, nf_g)


DEPTH_2 = 4

N_MIXERS = 3
SB_HEADS = 16
SB_HEAD_DIM = D_MODEL // SB_HEADS
SB_Q_BLOCK = 128
CONV_WIDTH = 3
GLA_HEADS = 4
GLA_DK = D_MODEL // 2
GLA_DV = D_MODEL
GLA_DK_HEAD = GLA_DK // GLA_HEADS
GLA_DV_HEAD = GLA_DV // GLA_HEADS
GLA_GATE_RANK = 16
GLA_GATE_NORMALIZER = 16.0
GLA_CHUNK = 64
D_FF_2 = 4 * D_MODEL
RMS_EPS = 1e-6


def rms_norm(x, gain):
    xf = x.astype(jnp.float32)
    y = xf * lax.rsqrt(jnp.mean(xf * xf, axis=-1, keepdims=True) + RMS_EPS) * gain.astype(jnp.float32)
    return y.astype(x.dtype)

def stick_breaking_mixer(xn, w_qkv, w_o):
    b, s, _ = xn.shape
    qkv = (xn @ w_qkv).reshape(b, s, 3, SB_HEADS, SB_HEAD_DIM)
    q, k, v = [qkv[:, :, i].transpose(0, 2, 1, 3).astype(jnp.float32) for i in range(3)]
    scale = SB_HEAD_DIM ** -0.5
    n_blocks = s // SB_Q_BLOCK
    q_blocks = q.reshape(b, SB_HEADS, n_blocks, SB_Q_BLOCK, SB_HEAD_DIM).transpose(2, 0, 1, 3, 4)
    key_pos = jnp.arange(s)

    def one_block(args):
        qb, start = args
        z = jnp.einsum('bhqd,bhkd->bhqk', qb, k) * scale
        q_pos = start + jnp.arange(SB_Q_BLOCK)
        mask = key_pos[None, :] < q_pos[:, None]
        log_beta = jax.nn.log_sigmoid(z)
        log_1m_beta = jnp.where(mask, jax.nn.log_sigmoid(-z), 0.0)
        suffix = lax.cumsum(log_1m_beta, axis=3, reverse=True) - log_1m_beta
        weights = jnp.where(mask, jnp.exp(log_beta + suffix), 0.0)
        return jnp.einsum('bhqk,bhkd->bhqd', weights, v)

    o = lax.map(one_block, (q_blocks, jnp.arange(n_blocks) * SB_Q_BLOCK))
    o = o.transpose(1, 0, 3, 2, 4).reshape(b, s, D_MODEL).astype(xn.dtype)
    return o @ w_o

def short_conv_mixer(xn, w_in, conv_w, w_out):
    s = xn.shape[1]
    bcu = xn @ w_in
    b_gate, c_gate, u = jnp.split(bcu, 3, axis=-1)
    h = c_gate * u
    hp = jnp.pad(h, ((0, 0), (CONV_WIDTH - 1, 0), (0, 0)))
    conv = sum(conv_w[i] * hp[:, i:i + s] for i in range(CONV_WIDTH))
    return (b_gate * conv) @ w_out

def gla_mixer(xn, w_in, w_gate_up, b_gate, head_norm, w_o):
    b, s, _ = xn.shape
    n_chunks = s // GLA_CHUNK
    proj = xn @ w_in
    q, k, v, g, a_low = jnp.split(
        proj, np.cumsum([GLA_DK, GLA_DK, GLA_DV, GLA_DV]).tolist(), axis=-1)
    log_gate = jax.nn.log_sigmoid(
        (a_low @ w_gate_up + b_gate).astype(jnp.float32)) / GLA_GATE_NORMALIZER

    def to_chunks(t, dh):
        t = t.astype(jnp.float32).reshape(b, n_chunks, GLA_CHUNK, GLA_HEADS, dh)
        return t.transpose(1, 0, 3, 2, 4)

    qc = to_chunks(q, GLA_DK_HEAD) * (GLA_DK_HEAD ** -0.5)
    kc = to_chunks(k, GLA_DK_HEAD)
    vc = to_chunks(v, GLA_DV_HEAD)
    gc = to_chunks(log_gate, GLA_DK_HEAD)
    causal = jnp.tril(jnp.ones((GLA_CHUNK, GLA_CHUNK), dtype=bool))

    def step(state, inp):
        qi, ki, vi, gi = inp
        cum = jnp.cumsum(gi, axis=2)
        inter = jnp.einsum('bhcd,bhde->bhce', qi * jnp.exp(cum), state)
        diff = cum[:, :, :, None, :] - cum[:, :, None, :, :]
        decay = jnp.exp(jnp.where(causal[None, None, :, :, None], diff, -jnp.inf))
        scores = jnp.einsum('bhid,bhjd,bhijd->bhij', qi, ki, decay)
        out = inter + jnp.einsum('bhij,bhje->bhie', scores, vi)
        last = cum[:, :, -1:, :]
        new_state = jnp.exp(last)[:, :, 0, :, None] * state + jnp.einsum(
            'bhcd,bhce->bhde', ki * jnp.exp(last - cum), vi)
        return new_state, out

    state0 = jnp.zeros((b, GLA_HEADS, GLA_DK_HEAD, GLA_DV_HEAD), jnp.float32)
    _, o = lax.scan(step, state0, (qc, kc, vc, gc))
    o = o.transpose(1, 0, 3, 2, 4).reshape(b, s, GLA_HEADS, GLA_DV_HEAD)
    o = rms_norm(o, head_norm).reshape(b, s, GLA_DV).astype(xn.dtype)
    return (o * jax.nn.silu(g)) @ w_o

def squared_relu_mlp(xn, w_up, w_down):
    return jnp.square(jax.nn.relu(xn @ w_up)) @ w_down

def second_inputs(seed: int = 0) -> dict:
    key = jax.random.key(seed)
    ks = jax.random.split(key, 16)
    n_sb = (DEPTH_2 + 2) // 3
    n_conv = (DEPTH_2 + 1) // 3
    n_gla = DEPTH_2 // 3
    f32 = jnp.float32

    def nrm(k, shape, scale):
        return jax.random.normal(k, shape, f32) * scale

    d_in_gla = 2 * GLA_DK + 2 * GLA_DV + GLA_GATE_RANK
    return {
        "x": nrm(ks[0], (BATCH, SEQ, D_MODEL), 1.0),
        "norm_gains": 1.0 + nrm(ks[1], (DEPTH_2, 4, D_MODEL), 0.02),
        "sb_w_qkv": nrm(ks[2], (n_sb, D_MODEL, 3 * D_MODEL), D_MODEL ** -0.5),
        "sb_w_o": nrm(ks[3], (n_sb, D_MODEL, D_MODEL), D_MODEL ** -0.5),
        "conv_w_in": nrm(ks[4], (n_conv, D_MODEL, 3 * D_MODEL), D_MODEL ** -0.5),
        "conv_w": nrm(ks[5], (n_conv, CONV_WIDTH, D_MODEL), CONV_WIDTH ** -0.5),
        "conv_w_out": nrm(ks[6], (n_conv, D_MODEL, D_MODEL), D_MODEL ** -0.5),
        "gla_w_in": nrm(ks[7], (n_gla, D_MODEL, d_in_gla), D_MODEL ** -0.5),
        "gla_w_gate_up": nrm(ks[8], (n_gla, GLA_GATE_RANK, GLA_DK), GLA_GATE_RANK ** -0.5),
        "gla_b_gate": nrm(ks[9], (n_gla, GLA_DK), 0.1),
        "gla_head_norm": 1.0 + nrm(ks[10], (n_gla, GLA_HEADS, GLA_DV_HEAD), 0.02),
        "gla_w_o": nrm(ks[11], (n_gla, GLA_DV, D_MODEL), GLA_DV ** -0.5),
        "ffn_w_up": nrm(ks[12], (DEPTH_2, D_MODEL, D_FF_2), D_MODEL ** -0.5),
        "ffn_w_down": nrm(ks[13], (DEPTH_2, D_FF_2, D_MODEL), D_FF_2 ** -0.5),
    }

def second_block(x, norm_gains, sb_w_qkv, sb_w_o, conv_w_in, conv_w, conv_w_out,
              gla_w_in, gla_w_gate_up, gla_b_gate, gla_head_norm, gla_w_o,
              ffn_w_up, ffn_w_down):
    h = x
    for i in range(DEPTH_2):
        kind, j = i % N_MIXERS, i // N_MIXERS
        xn = rms_norm(h, norm_gains[i, 0])
        if kind == 0:
            m = stick_breaking_mixer(xn, sb_w_qkv[j], sb_w_o[j])
        elif kind == 1:
            m = short_conv_mixer(xn, conv_w_in[j], conv_w[j], conv_w_out[j])
        else:
            m = gla_mixer(xn, gla_w_in[j], gla_w_gate_up[j], gla_b_gate[j],
                          gla_head_norm[j], gla_w_o[j])
        h = h + rms_norm(m, norm_gains[i, 1])
        f = squared_relu_mlp(rms_norm(h, norm_gains[i, 2]), ffn_w_up[i], ffn_w_down[i])
        h = h + rms_norm(f, norm_gains[i, 3])
    return h


def setup_inputs(seed=0):
    out = dict(first_inputs(seed))
    for name, value in second_inputs(seed + 1).items():
        if name != "x":
            out[name + "_2"] = value
    return out


def reference(
    x, n1_g, ffn1_w_in, ffn1_w_out, n2_g, w_in, rel_bias, w_branch_a, w_branch_b, w_out, n3_g,
    ffn2_w_in, ffn2_w_out, nf_g, norm_gains_2, sb_w_qkv_2, sb_w_o_2, conv_w_in_2, conv_w_2,
    conv_w_out_2, gla_w_in_2, gla_w_gate_up_2, gla_b_gate_2, gla_head_norm_2, gla_w_o_2,
    ffn_w_up_2, ffn_w_down_2,
):
    x = first_block(
        x, n1_g, ffn1_w_in, ffn1_w_out, n2_g, w_in, rel_bias, w_branch_a, w_branch_b, w_out,
        n3_g, ffn2_w_in, ffn2_w_out, nf_g,
    )
    return second_block(
        x, norm_gains_2, sb_w_qkv_2, sb_w_o_2, conv_w_in_2, conv_w_2, conv_w_out_2, gla_w_in_2,
        gla_w_gate_up_2, gla_b_gate_2, gla_head_norm_2, gla_w_o_2, ffn_w_up_2, ffn_w_down_2,
    )


_drawn_inputs = setup_inputs


def setup_inputs(seed=0):
    import zlib

    import numpy as np

    out = dict(_drawn_inputs(seed))
    spreads = {}
    factors = {'n3_g': 3.928, 'gla_b_gate_2': 3.127, 'gla_head_norm_2': 6.81}
    for name, (base, spread) in spreads.items():
        noise = np.random.default_rng([zlib.crc32(name.encode()), seed]).standard_normal(out[name].shape)
        drawn = base * np.exp(spread * noise) if base else spread * noise
        out[name] = __import__('jax').numpy.asarray(drawn.astype(out[name].dtype))
    for name, factor in factors.items():
        out[name] = (out[name] * factor).astype(out[name].dtype)
    return out
```

```python
from contextlib import ExitStack

import numpy as np

import concourse.bass as bass
from concourse import mybir

F32 = mybir.dt.float32
F32R = mybir.dt.float32r
ALU = mybir.AluOpType
ACT = mybir.ActivationFunctionType
AX_X = mybir.AxisListType.X

P = 128
SEQ = 256
NT = SEQ // P
D = 1024
KT = D // P
BANK = 512
PANELS = 4
PART = PANELS * BANK
EPS = 1e-6
FAR = -1.0e30
TAKEN = -3.0e38

FF1 = 2816
FF1_STEP = 256
FF1_ITERS = FF1 // FF1_STEP
FF2 = 4096
FF2_STEP = 512
FF2_ITERS = FF2 // FF2_STEP
DEPTH2 = 4

C_QB, C_QI, C_KB, C_KI, C_VB, C_WI = 0, 512, 1024, 1152, 1280, 1408
C_QA, C_KA, C_VA, C_GA, C_GB = 1536, 2048, 2560, 3072, 4096
PCOLS = 5120
ROPE_HEADS = 20
TOPK = 64
SPAN = 384

K_ID, K_ONES, K_GT, K_LT, K_LE, K_COS, K_SIN, KCOLS = 0, 128, 256, 384, 512, 576, 608, 640

ARENA = 6656
QK_BANKS = {"mix_ab": 9, "mix_sb": 8, "mix_conv": 8, "mix_gla": 4}


def stage_list():
    st = []
    cnt = {}

    def add(kind, **kw):
        kw["kind"] = kind
        st.append(kw)
        return kw

    def norm(to="y"):
        add("norm", to=to)

    norm(); add("trans"); add("gated"); add("add", scale=0.5)
    norm(); add("trans"); add("lin", doubles=5); add("mix_ab"); add("branch")
    add("trans"); add("out"); add("add", scale=1.0)
    norm(); add("trans"); add("gated"); add("add", scale=0.5)
    norm(to="x")
    for layer in range(DEPTH2):
        norm(); add("trans")
        kind = layer % 3
        add("lin", doubles=3)
        if kind == 0:
            add("mix_sb")
        elif kind == 1:
            add("mix_conv")
        else:
            add("mix_gla"); add("trans")
        add("out"); add("addnorm")
        norm(); add("trans"); add("squared"); add("addnorm")
    add("store")

    run = {k: 0 for k in ("gain", "y", "xt", "x", "acc", "lin", "tr", "up", "sq", "gt", "stat",
                          "norm", "add", "sb", "part", "qk", "qka", "qkd")}
    for s in st:
        s.update({"n_" + k: v for k, v in run.items()})
        kind = s["kind"]
        if kind in QK_BANKS:
            run["qk"] += QK_BANKS[kind]
            run["qka"] += (QK_BANKS[kind] + 1) // 2
            run["qkd"] += QK_BANKS[kind] // 2
        if kind in ("norm", "addnorm"):
            run["gain"] += 1
            run["stat"] += 1
        if kind == "norm":
            run["norm"] += 1
            run["x" if s["to"] == "x" else "y"] += 1
        elif kind == "addnorm":
            run["add"] += 1
            run["x"] += 1
        elif kind == "add":
            run["x"] += 1
        elif kind == "trans":
            run["tr"] += 1
            run["xt"] += 1
        elif kind == "lin":
            run["lin"] += 2 * s["doubles"]
            run["part"] += 4 * s["doubles"]
        elif kind == "out":
            run["acc"] += 1
            run["part"] += 4
        elif kind == "branch":
            run["y"] += 1
            run["part"] += 4
        elif kind == "mix_ab":
            run["xt"] += 1
        elif kind == "mix_sb":
            run["xt"] += 1
            run["sb"] += 1
        elif kind == "mix_conv":
            run["xt"] += 1
        elif kind == "mix_gla":
            run["y"] += 1
            run["gain"] += 1
            run["stat"] += 1
        elif kind == "gated":
            run["acc"] += 1
            run["up"] += FF1_ITERS
            run["gt"] += FF1_ITERS
            run["part"] += 3 * FF1_ITERS
        elif kind == "squared":
            run["acc"] += 1
            run["up"] += FF2_ITERS
            run["sq"] += FF2_ITERS
            run["part"] += 4 * FF2_ITERS
    return st, run


def constants():
    c = np.zeros((P, KCOLS), np.float32)
    p = np.arange(P)[:, None]
    f = np.arange(P)[None, :]
    c[:, K_ID:K_ID + P] = p == f
    c[:, K_ONES:K_ONES + P] = 1.0
    c[:, K_GT:K_GT + P] = p > f
    c[:, K_LT:K_LT + P] = p < f
    c[:, K_LE:K_LE + 64] = (p % 64) <= f[:, :64]
    inv = np.power(np.float32(500000.0), -np.arange(0, 16, 2, dtype=np.float32) / np.float32(16)).astype(np.float32)
    ang = (np.arange(SEQ, dtype=np.float32)[:, None] * inv[None, :]).astype(np.float32)
    cos = np.cos(ang).astype(np.float32).reshape(NT, P, 8)
    sin = np.sin(ang).astype(np.float32).reshape(NT, P, 8)
    for t in range(NT):
        c[:, K_COS + 16 * t:K_COS + 16 * t + 16] = np.concatenate([cos[t], cos[t]], 1)
        c[:, K_SIN + 16 * t:K_SIN + 16 * t + 16] = np.concatenate([-sin[t], sin[t]], 1)
    return c


def build(nc, x_in, w_parts, gains, const_in, bias_line, conv_w, gla_low, gla_up, gla_b, out):
    STAGES, TOTAL = stage_list()

    with ExitStack() as ctx:
        def sb(name, shape, dt=F32):
            return ctx.enter_context(nc.sbuf_tensor(name, shape, dt))

        def sem(name):
            return ctx.enter_context(nc.semaphore(name))

        raw = [sb(f"raw{s}", [P, PART]) for s in range(4)]
        whi = [sb(f"whi{s}", [P, PART], F32R) for s in range(4)]
        wlo = [sb(f"wlo{s}", [P, PART], F32R) for s in range(4)]
        x = sb("x", [P, NT, D])
        xhi = sb("xhi", [P, KT, SEQ], F32R)
        xlo = sb("xlo", [P, KT, SEQ], F32R)
        hhi = sb("hhi", [P, NT, 4, P], F32R)
        hlo = sb("hlo", [P, NT, 4, P], F32R)
        proj = sb("proj", [P, NT, PCOLS])
        gain = sb("gain", [P, 2, D])
        const = sb("const", [P, KCOLS])
        cw = sb("cw", [P, KT, 3])
        wlow = sb("wlow", [P, KT, 16])
        wup = sb("wup", [16, 512])
        bgate = sb("bgate", [P, 4])
        stat = sb("stat", [P, 8, 8])
        wsc = sb("wsc", [P, NT, 8])
        top8 = sb("top8", [P, NT, 8])
        unit_stat = sb("unit_stat", [P, 4, 2, 2])
        arena = sb("arena", [P, ARENA])
        ps = ctx.enter_context(nc.psum_tensor("ps", [P, 8, BANK], F32))

        ident = const[:, K_ID:K_ID + P]
        Y = arena[:, 0:2048].rearrange("p (t d) -> p t d", t=NT)
        R = arena[:, 2048:3072].rearrange("p (t f) -> p t f", t=NT)
        H = arena[:, 3072:4096].rearrange("p (t f) -> p t f", t=NT)
        EG = arena[:, 4096:4608].rearrange("p (t f) -> p t f", t=NT)

        BIAS = arena[:, 4608:6656].rearrange("p (h k) -> p h k", h=8)
        ROPE_A = arena[:, 3584:3904].rearrange("p (h e) -> p h e", e=16)
        ROPE_B = arena[:, 3904:4224].rearrange("p (h e) -> p h e", e=16)
        REL = [proj[:, 0, 0:384], proj[:, 0, 384:768]]
        IXS = proj[:, 0, 768:1152]
        MSK = proj[:, 1, 0:384]
        SC = [proj[:, 0, 1536:1920], proj[:, 0, 1920:2304]]
        PTB = [proj[:, 1, 1536:1920], proj[:, 1, 1920:2304]]
        spare = [arena[:, 4096 + SPAN * i:4096 + SPAN * (i + 1)] for i in range(6)]
        spare += [proj[:, t, 3072 + SPAN * i:3072 + SPAN * (i + 1)] for t in range(NT) for i in range(5)]
        SA, SN, SL, SW = spare[0:4], spare[4:8], spare[8:12], spare[12:16]
        BT = arena[:, 0:2048].rearrange("p (k n) -> p k n", k=KT)
        HT = arena[:, 2048:4112].rearrange("p (k n) -> p k n", k=KT)
        AC = arena[:, 4112:6160].rearrange("p (k n) -> p k n", k=KT)
        GQK = arena[:, 0:2048]
        GC = arena[:, 2048:3072]
        GL = arena[:, 3072:4096]
        GQX = arena[:, 4096:5120]
        GQI = arena[:, 5120:6144]
        LOW = arena[:, 6144:6400]
        EL = arena[:, 6400:6416]
        GKN, GST = GQK[:, 0:1024], GL
        GK = [proj[:, 0, 3072:3328], proj[:, 0, 3328:3840], proj[:, 0, 3840:4608], proj[:, 1, 3072:4096]]
        GKS = proj[:, 1, 4096:5120]
        GS = proj[:, 0, 4608:5120]

        def acc_tile(t):
            return ps[:, 2 * t:2 * t + 2, :].rearrange("p b n -> p (b n)")

        raw_in = [sem(f"raw_in{s}") for s in range(4)]
        hi_ready = [sem(f"hi_ready{s}") for s in range(4)]
        lo_ready = [sem(f"lo_ready{s}") for s in range(4)]
        w_used = [sem(f"w_used{s}") for s in range(4)]
        x_in_sem = sem("x_in")
        const_sem = sem("const_in")
        small_sem = sem("small_in")
        bias_sem = sem("bias_in")
        gain_in = [sem("gain_in0"), sem("gain_in1")]
        gain_used = sem("gain_used")
        x_ready = sem("x_ready")
        sum_ready = sem("sum_ready")
        var_ready = sem("var_ready")
        log_ready = sem("log_ready")
        rs_ready = sem("rs_ready")
        y_ready = sem("y_ready")
        tr_ready = sem("tr_ready")
        xhi_ready = sem("xhi_ready")
        xlo_ready = sem("xlo_ready")
        lin_ready = sem("lin_ready")
        lin_evac = sem("lin_evac")
        acc_ready = sem("acc_ready")
        up_ready = sem("up_ready")
        relu_ready = sem("relu_ready")
        gexp_ready = sem("gexp_ready")
        gden_ready = sem("gden_ready")
        grec_ready = sem("grec_ready")
        gact_ready = sem("gact_ready")
        h_ready = sem("h_ready")
        ht_ready = sem("ht_ready")
        hhi_ready = sem("hhi_ready")
        hlo_ready = sem("hlo_ready")
        qk_tr = sem("qk_tr")
        qk_act = sem("qk_act")
        qk_dve = sem("qk_dve")
        dve_step = sem("dve_step")
        act_step = sem("act_step")
        pool_step = sem("pool_step")
        rope_done = sem("rope_done")
        ix_ready = sem("ix_ready")
        ix_relu = sem("ix_relu")
        ix_acc = sem("ix_acc")
        sig_exp = sem("sig_exp")
        sig_den = sem("sig_den")
        score_ready = sem("score_ready")
        biased = sem("biased")
        nmax_ready = sem("nmax_ready")
        p_exp = sem("p_exp")
        rden_ready = sem("rden_ready")
        p_ready = sem("p_ready")
        ptr_ready = sem("ptr_ready")
        pt_ready = sem("pt_ready")
        pv_ready = sem("pv_ready")
        br_ready = sem("br_ready")
        z_ready = sem("z_ready")
        l_ready = sem("l_ready")
        sp_ready = sem("sp_ready")
        lb_ready = sem("lb_ready")
        spm_ready = sem("spm_ready")
        suf_ready = sem("suf_ready")
        arg_ready = sem("arg_ready")
        w_exp = sem("w_exp")
        w_ready = sem("w_ready")
        sbpv_ready = sem("sbpv_ready")
        cu_dve = sem("cu_dve")
        cu_pool = sem("cu_pool")
        tap0_ready = sem("tap0_ready")
        conv_ready = sem("conv_ready")
        low_ready = sem("low_ready")
        low_sb = sem("low_sb")
        gate_ps = sem("gate_ps")
        gz_ready = sem("gz_ready")
        gl_ready = sem("gl_ready")
        cum_ready = sem("cum_ready")
        gdiff_ready = sem("gdiff_ready")
        gx_ready = sem("gx_ready")
        qk_scaled = sem("qk_scaled")
        qk_pool = sem("qk_pool")
        gs_ready = sem("gs_ready")
        gs_sb = sem("gs_sb")
        kn_ps = sem("kn_ps")
        kn_sb = sem("kn_sb")
        upd_ready = sem("upd_ready")
        state_ready = sem("state_ready")
        go_ready = sem("go_ready")
        swish_exp = sem("swish_exp")
        swish_den = sem("swish_den")
        swish_ready = sem("swish_ready")
        out_done = sem("out_done")

        GAINS = TOTAL["gain"]

        class Slots:
            def __init__(self):
                self.n = [0, 0, 0, 0]

            def take(self, s):
                self.n[s] += 1
                return self.n[s] - 1

        class Steps:
            def __init__(self, eng, s):
                self.eng, self.s, self.n = eng, s, 0

            def __call__(self, ins):
                self.n += 1
                ins.then_inc(self.s, 1)
                self.eng.wait_ge(self.s, self.n)

        block = ctx.enter_context(nc.Block())

        @block.sync
        def _(sp):
            slots = Slots()
            gains_sent = [0]
            state = {"part": 0}

            def load_part(s, part, n):
                if not isinstance(n, int) or n >= 1:
                    sp.wait_ge(lo_ready[s], n)
                sp.dma_start(raw[s][:], w_parts[bass.ds(part, 1), :, :].rearrange("a p n -> (a p) n")
                             ).then_inc(raw_in[s], 16)

            def load_parts(slot_ids):
                for s in slot_ids:
                    load_part(s, state["part"], slots.take(s))
                    state["part"] += 1

            def loop_parts(slot_ids, first, last):
                base, part0 = list(slots.n), state["part"]
                with sp.Fori(first, last) as i:
                    for j, s in enumerate(slot_ids):
                        load_part(s, (i - first) * len(slot_ids) + (part0 + j), (i - first) + base[s])
                for s in slot_ids:
                    slots.n[s] += last - first
                state["part"] += (last - first) * len(slot_ids)

            def load_gains(upto):
                while gains_sent[0] < min(upto, GAINS):
                    q = gains_sent[0]
                    if q >= 2:
                        sp.wait_ge(gain_used, q - 1)
                    sp.dma_start(gain[:, q % 2, :], gains[q:q + 1, :].to_broadcast([P, D])
                                 ).then_inc(gain_in[q % 2], 16)
                    gains_sent[0] += 1

            load_gains(2)
            for s in STAGES:
                kind = s["kind"]
                if kind == "gated":
                    load_parts([0, 1, 2])
                    load_parts([0, 1, 2])
                    load_gains(s["n_gain"] + 2)
                    loop_parts([0, 1, 2], 2, FF1_ITERS)
                elif kind == "squared":
                    load_parts([0, 1, 2, 3])
                    load_parts([0, 1, 2, 3])
                    load_gains(s["n_gain"] + 2)
                    loop_parts([0, 1, 2, 3], 2, FF2_ITERS)
                elif kind == "lin":
                    load_parts([0, 1, 2, 3])
                    load_gains(s["n_gain"] + 2)
                    loop_parts([0, 1, 2, 3], 1, s["doubles"])
                elif kind in ("out", "branch"):
                    load_parts([0, 1, 2, 3])
                    load_gains(s["n_gain"] + 2)
                elif kind == "store":
                    sp.wait_ge(x_ready, NT * s["n_x"])
                    for t in range(NT):
                        sp.dma_start(out[t * P:(t + 1) * P, :], x[:, t, :]).then_inc(out_done, 16)
                    sp.wait_ge(out_done, 16 * NT)

        @block.scalar
        def _(act):
            slots = Slots()
            step = Steps(act, act_step)
            early = {"done": -1}

            act.dma_start(x[:], x_in.rearrange("(t p) d -> p t d", p=P)).then_inc(x_in_sem, 16)
            act.dma_start(const[:], const_in).then_inc(const_sem, 16)
            for dst, src in ((cw[:], conv_w), (wlow[:], gla_low), (wup[:], gla_up), (bgate[:], gla_b)):
                act.dma_start(dst, src).then_inc(small_sem, 16)

            def split_hi(s, n):
                act.wait_ge(raw_in[s], (n + 1) * 16)
                if not isinstance(n, int) or n >= 1:
                    act.wait_ge(w_used[s], n)
                nc.scalar.activation(whi[s][:], raw[s][:], ACT.Copy).then_inc(hi_ready[s], 1)

            def split_next(ids):
                for s in ids:
                    split_hi(s, slots.take(s))

            def split_early(index):
                for j in range(index + 1, len(STAGES)):
                    if STAGES[j]["kind"] in ("gated", "squared", "lin", "out", "branch"):
                        split_next([0, 1])
                        STAGES[j].setdefault("early", set()).add("act")
                        return

            def row_stat_log(s):
                act.wait_ge(var_ready, s["n_stat"] + 1)
                cols = s.get("cols", NT)
                nc.scalar.activation(stat[:, 2, 0:cols], stat[:, 1, 0:cols], ACT.Ln).then_inc(log_ready, 1)
                act.wait_ge(log_ready, s["n_stat"] + 1)
                nc.scalar.activation(stat[:, 3, 0:cols], stat[:, 2, 0:cols], ACT.Exp, scale=-0.5).then_inc(rs_ready, 1)

            sums = [0]

            def ffn(index, s, iters, gated):
                dslots = [2] if gated else [2, 3]
                up0 = s["n_up"]
                kt = 2 if gated else 4

                def hidden_hi(i):
                    act.wait_ge(ht_ready, i + (up0 + 1))
                    nc.scalar.activation(hhi[:, :, 0:kt, :], ps[:, 6:8, 0:kt * P].rearrange("p t (k n) -> p t k n", k=kt),
                                         ACT.Copy).then_inc(hhi_ready, 1)

                def activate(i):
                    act.wait_ge(up_ready, i + (up0 + 1))
                    if gated:
                        if not isinstance(i, int) or i >= 1:
                            act.wait_ge(h_ready, i + up0)
                        nc.scalar.activation(EG[:], ps[:, 4:6, 0:FF1_STEP], ACT.Exp, scale=-1.0).then_inc(gexp_ready, 1)
                    else:
                        if not isinstance(i, int) or i >= 1:
                            act.wait_ge(h_ready, i + up0)
                        nc.scalar.activation(R[:], ps[:, 4:6, :], ACT.Relu).then_inc(relu_ready, 1)

                def body(i, n):
                    for q in (0, 1):
                        split_hi(q, n[q])
                    hidden_hi(i - 1)
                    for q in dslots:
                        split_hi(q, n[q])
                    activate(i)

                if "act" not in s.get("early", ()):
                    split_next([0, 1])
                activate(0)
                body(1, {q: slots.take(q) for q in [0, 1] + dslots})
                base = list(slots.n)
                with act.Fori(2, iters) as i:
                    body(i, {q: (i - 2) + base[q] for q in [0, 1] + dslots})
                for q in [0, 1] + dslots:
                    slots.n[q] += iters - 2
                hidden_hi(iters - 1)
                split_next(dslots)
                split_early(index)

            def lin(index, s):
                base = s["n_lin"]

                def evac(j, col):
                    act.wait_ge(lin_ready, j + (base + 1))
                    b = 4 + 2 * col
                    nc.scalar.activation(proj[:, :, bass.ds(j * BANK, BANK)], ps[:, b:b + 2, :], ACT.Copy).then_inc(lin_evac, 1)

                if "act" not in s.get("early", ()):
                    split_next([0, 1])
                n0 = list(slots.n)
                with act.Fori(0, s["doubles"] - 1) as d:
                    for q in (2, 3):
                        split_hi(q, d + n0[q])
                    evac(d * 2, 0)
                    for q in (0, 1):
                        split_hi(q, d + n0[q])
                    evac(d * 2 + 1, 1)
                for q in range(4):
                    slots.n[q] += s["doubles"] - 1
                last = 2 * (s["doubles"] - 1)
                split_next([2, 3])
                evac(last, 0)
                split_early(index)
                evac(last + 1, 1)

            def trans_hi(s):
                for b in range(4):
                    t, half = b // 2, b % 2
                    act.wait_ge(tr_ready, 4 * s["n_tr"] + b + 1)
                    nc.scalar.activation(xhi[:, 4 * half:4 * half + 4, t * P:(t + 1) * P],
                                         ps[:, b, :].rearrange("p (k n) -> p k n", k=4), ACT.Copy).then_inc(xhi_ready, 1)

            def copy_t(base, b, scale=1.0, dst=None):
                act.wait_ge(qk_tr, base + b + 1)
                d = dst if dst is not None else arena[:, b * BANK:(b + 1) * BANK]
                return nc.scalar.activation(d, ps[:, b % 4, :], ACT.Copy, scale=scale).then_inc(qk_act, 1)

            def mix_ab(s):
                act.wait_ge(lin_evac, s["n_lin"])
                g = proj[:, :, C_GA:C_GA + 2 * D]
                nc.scalar.activation(g, g, ACT.Exp, scale=-1.0).then_inc(sig_exp, 1)
                for b in range(0, 9, 2):
                    copy_t(0, b)
                for h in range(8):
                    act.wait_ge(ix_ready, h + 1)
                    if h >= 2:
                        act.wait_ge(ix_acc, h - 1)
                    nc.scalar.activation(REL[h % 2], ps[:, 4 + h % 4, 0:SPAN], ACT.Relu, scale=0.125).then_inc(ix_relu, 1)

                def exps(u):
                    act.wait_ge(nmax_ready, u + 1)
                    for t, (a, b) in enumerate(((256, 384), (0, 256))):
                        ins = nc.scalar.activation(SC[u % 2][:, a:b], SC[u % 2][:, a:b], ACT.Exp,
                                                   bias=unit_stat[:, 1, u % 2, t:t + 1],
                                                   accum_out=unit_stat[:, 2, u % 2, t:t + 1])
                    ins.then_inc(p_exp, 1)

                def pt_copy(u):
                    act.wait_ge(ptr_ready, u + 1)
                    if u >= 2:
                        act.wait_ge(pv_ready, u - 1)
                    nc.scalar.activation(PTB[u % 2], ps[:, 6 + u % 2, 0:SPAN], ACT.Copy).then_inc(pt_ready, 1)

                def o_hi(b):
                    act.wait_ge(pv_ready, 4 * b + 4)
                    nc.scalar.activation(xhi[:, 2 * b:2 * b + 2, :], ps[:, b, :].rearrange("p (k n) -> p k n", k=2),
                                         ACT.Copy).then_inc(xhi_ready, 1)

                for u in range(18):
                    if u < 16:
                        exps(u)
                    if 1 <= u < 17:
                        pt_copy(u - 1)
                    if u >= 2 and (u - 2) % 4 == 3:
                        o_hi((u - 2) // 4)

            def mix_sb(s):
                r = s["n_sb"]
                base = s["n_qk"]
                for b in range(0, 8, 2):
                    copy_t(base, b, scale=0.125 if b < 4 else 1.0)
                u0 = 16 * r
                for u in range(18):
                    if u < 16:
                        act.wait_ge(z_ready, u0 + u + 1)
                        if u >= 4:
                            act.wait_ge(lb_ready, u0 + u - 3)
                        step(nc.scalar.activation(SA[u % 4], ps[:, 4 + u % 2, 0:SPAN], ACT.Abs))
                        step(nc.scalar.activation(SA[u % 4], SA[u % 4], ACT.Exp, scale=-1.0))
                        nc.scalar.activation(SA[u % 4], SA[u % 4], ACT.Ln, bias=1.0).then_inc(l_ready, 1)
                    v = u - 2
                    if v >= 0:
                        act.wait_ge(arg_ready, u0 + v + 1)
                        nc.scalar.activation(SW[v % 4], SW[v % 4], ACT.Exp).then_inc(w_exp, 1)
                    if v >= 2 and (v - 2) % 4 == 3:
                        sb_o_hi(u0, (v - 2) // 4)
                sb_o_hi(u0, 3)

            def sb_o_hi(u0, b):
                act.wait_ge(sbpv_ready, u0 + 4 * b + 4)
                nc.scalar.activation(xhi[:, 2 * b:2 * b + 2, :], ps[:, b, :].rearrange("p (k n) -> p k n", k=2),
                                     ACT.Copy).then_inc(xhi_ready, 1)

            def mix_conv(s):
                base = s["n_qk"]
                for b in range(0, 8, 2):
                    if b < 4:
                        copy_t(base, b, dst=BT[:, 2 * b:2 * b + 2, :].rearrange("p k n -> p (k n)"))
                    else:
                        act.wait_ge(qk_tr, base + b + 1)
                        nc.scalar.activation(HT[:, 2 * b - 8:2 * b - 6, 2:258], ps[:, b % 4, :].rearrange("p (k n) -> p k n", k=2),
                                             ACT.Copy).then_inc(qk_act, 1)
                act.wait_ge(small_sem, 64)
                for k in range(KT):
                    if k % 4 == 0:
                        act.wait_ge(qk_act, s["n_qka"] + 3 + k // 4)
                        act.wait_ge(qk_dve, s["n_qkd"] + 3 + k // 4)
                    nc.scalar.activation(AC[:, k, :], HT[:, k, 0:256], ACT.Copy, scale=cw[:, k, 0:1]).then_inc(tap0_ready, 1)
                for b in range(4):
                    act.wait_ge(conv_ready, 2 * b + 2)
                    nc.scalar.activation(xhi[:, 2 * b:2 * b + 2, :], AC[:, 2 * b:2 * b + 2, :], ACT.Copy).then_inc(xhi_ready, 1)

            def mix_gla(s):
                base = s["n_qk"]
                act.wait_ge(low_ready, 1)
                nc.scalar.activation(LOW[0:16, :], ps[0:16, 4, 0:SEQ], ACT.Copy).then_inc(low_sb, 1)
                for b in range(0, 4, 2):
                    copy_t(base, b, scale=128.0 ** -0.5 if b < 2 else 1.0, dst=GQK[:, b * BANK:(b + 1) * BANK])
                act.wait_ge(lin_evac, s["n_lin"])
                act.wait_ge(qk_tr, base + 4)
                nc.scalar.activation(proj[:, :, 0:D], proj[:, :, 2 * D:3 * D], ACT.Exp, scale=-1.0).then_inc(swish_exp, 1)
                act.wait_ge(gz_ready, 1)
                step(nc.scalar.activation(GL, GC, ACT.Abs))
                step(nc.scalar.activation(GL, GL, ACT.Exp, scale=-1.0))
                nc.scalar.activation(GL, GL, ACT.Ln, bias=1.0).then_inc(gl_ready, 1)
                act.wait_ge(cum_ready, 1)
                nc.scalar.activation(GQI, GC, ACT.Exp).then_inc(gx_ready, 1)
                act.wait_ge(gdiff_ready, 1)
                nc.scalar.activation(GQX, GQX, ACT.Exp).then_inc(gx_ready, 1)
                for a in range(4):
                    act.wait_ge(gdiff_ready, 2 + a)
                    nc.scalar.activation(GK[a], GK[a], ACT.Exp).then_inc(gx_ready, 1)
                act.wait_ge(gdiff_ready, 6)
                nc.scalar.activation(GKS, GKS, ACT.Exp).then_inc(gx_ready, 1)
                act.wait_ge(gdiff_ready, 7)
                nc.scalar.activation(EL[:], EL[:], ACT.Exp).then_inc(gx_ready, 1)
                for b in range(2):
                    act.wait_ge(kn_ps, b + 1)
                    nc.scalar.activation(GKN[:, b * BANK:(b + 1) * BANK], ps[:, 6 + b, :], ACT.Copy).then_inc(kn_sb, 1)
                act.wait_ge(go_ready, 1)
                for t in range(NT):
                    for h in range(4):
                        ins = nc.scalar.activation(GQI[:, 0:256], acc_tile(t)[:, h * 256:(h + 1) * 256], ACT.Square,
                                                   accum_out=stat[:, 0, 4 * t + h:4 * t + h + 1])
                        if not (t == 1 and h == 3):
                            step(ins)
                sums[0] += 1
                ins.then_inc(sum_ready, 1)
                row_stat_log(dict(s, cols=8))

            for index, s in enumerate(STAGES):
                kind = s["kind"]
                if kind == "norm":
                    if s["n_x"] == 0:
                        if s["n_norm"] == 0:
                            act.wait_ge(x_in_sem, 16)
                    else:
                        act.wait_ge(x_ready, NT * (s["n_x"] - 1) + 1)
                    nc.scalar.activation(Y[:, 0, :], x[:, 0, :], ACT.Square, accum_out=stat[:, 0, 0:1]).then_inc(sum_ready, 1)
                    row_stat_log(s)
                elif kind == "addnorm":
                    act.wait_ge(acc_ready, s["n_acc"])
                    step(nc.scalar.activation(Y[:, 0, :], acc_tile(0), ACT.Square, accum_out=stat[:, 0, 0:1]))
                    nc.scalar.activation(Y[:, 1, :], acc_tile(1), ACT.Square, accum_out=stat[:, 0, 1:2]).then_inc(sum_ready, 1)
                    row_stat_log(s)
                elif kind == "trans":
                    trans_hi(s)
                elif kind == "gated":
                    ffn(index, s, FF1_ITERS, True)
                elif kind == "squared":
                    ffn(index, s, FF2_ITERS, False)
                elif kind == "lin":
                    lin(index, s)
                elif kind == "out":
                    if "act" not in s.get("early", ()):
                        split_next([0, 1])
                    split_next([2, 3])
                    split_early(index)
                elif kind == "branch":
                    if "act" not in s.get("early", ()):
                        split_next([0, 1])
                    split_next([2, 3])
                    split_early(index)
                elif kind == "mix_ab":
                    mix_ab(s)
                elif kind == "mix_sb":
                    mix_sb(s)
                elif kind == "mix_conv":
                    mix_conv(s)
                elif kind == "mix_gla":
                    mix_gla(s)

        @block.vector
        def _(dve):
            slots = Slots()
            step = Steps(dve, dve_step)

            def split_lo(s, n):
                dve.wait_ge(hi_ready[s], n + 1)
                nc.vector.tensor_tensor(wlo[s][:], raw[s][:], whi[s][:].bitcast(F32), ALU.subtract).then_inc(lo_ready[s], 1)

            def split_next(ids):
                for s in ids:
                    split_lo(s, slots.take(s))

            def split_early(index):
                for j in range(index + 1, len(STAGES)):
                    if STAGES[j]["kind"] in ("gated", "squared", "lin", "out", "branch"):
                        split_next([0, 1])
                        STAGES[j].setdefault("early", set()).add("dve")
                        return

            def row_stat(s, width, cols=NT):
                dve.wait_ge(sum_ready, s["n_stat"] + 1)
                nc.vector.tensor_scalar(stat[:, 1, 0:cols], stat[:, 0, 0:cols], 1.0 / width, EPS, ALU.mult, ALU.add
                                        ).then_inc(var_ready, 1)
                dve.wait_ge(rs_ready, s["n_stat"] + 1)
                step(nc.vector.tensor_tensor(stat[:, 4, 0:cols], stat[:, 3, 0:cols], stat[:, 3, 0:cols], ALU.mult))
                step(nc.vector.tensor_tensor(stat[:, 5, 0:cols], stat[:, 4, 0:cols], stat[:, 1, 0:cols], ALU.mult))
                step(nc.vector.tensor_scalar(stat[:, 6, 0:cols], stat[:, 5, 0:cols], -0.5, 1.5, ALU.mult, ALU.add))
                step(nc.vector.tensor_tensor(stat[:, 7, 0:cols], stat[:, 6, 0:cols], stat[:, 3, 0:cols], ALU.mult))
                q = s["n_gain"]
                dve.wait_ge(gain_in[q % 2], 16 * (q // 2 + 1))

            def ffn(index, s, iters, gated):
                dslots = [2] if gated else [2, 3]
                up0, gt0 = s["n_up"], s["n_gt"]
                kt = 2 if gated else 4

                def hidden_lo(i):
                    dve.wait_ge(hhi_ready, i + (up0 + 1))
                    nc.vector.tensor_tensor(hlo[:, :, 0:kt, :], ps[:, 6:8, 0:kt * P].rearrange("p t (k n) -> p t k n", k=kt),
                                            hhi[:, :, 0:kt, :].bitcast(F32), ALU.subtract).then_inc(hlo_ready, 1)

                def gate(i):
                    if not gated:
                        return
                    dve.wait_ge(gden_ready, i + (gt0 + 1))
                    nc.vector.reciprocal(EG[:], EG[:]).then_inc(grec_ready, 1)
                    dve.wait_ge(grec_ready, i + (gt0 + 1))
                    nc.vector.tensor_tensor(R[:, :, 0:FF1_STEP], ps[:, 4:6, 0:FF1_STEP], EG[:], ALU.mult).then_inc(gact_ready, 1)
                    dve.wait_ge(gact_ready, i + (gt0 + 1))
                    nc.vector.tensor_tensor(H[:, :, 0:FF1_STEP], ps[:, 4:6, FF1_STEP:2 * FF1_STEP], R[:, :, 0:FF1_STEP],
                                            ALU.mult).then_inc(h_ready, 1)

                def body(i, n):
                    for q in (0, 1):
                        split_lo(q, n[q])
                    hidden_lo(i - 1)
                    for q in dslots:
                        split_lo(q, n[q])
                    gate(i)

                if "dve" not in s.get("early", ()):
                    split_next([0, 1])
                gate(0)
                body(1, {q: slots.take(q) for q in [0, 1] + dslots})
                base = list(slots.n)
                with dve.Fori(2, iters) as i:
                    body(i, {q: (i - 2) + base[q] for q in [0, 1] + dslots})
                for q in [0, 1] + dslots:
                    slots.n[q] += iters - 2
                hidden_lo(iters - 1)
                split_next(dslots)
                split_early(index)

            def lin(index, s):
                if "dve" not in s.get("early", ()):
                    split_next([0, 1])
                n0 = list(slots.n)
                with dve.Fori(0, s["doubles"] - 1) as d:
                    for q in (2, 3, 0, 1):
                        split_lo(q, d + n0[q])
                for q in range(4):
                    slots.n[q] += s["doubles"] - 1
                split_next([2, 3])
                split_early(index)

            def x_lo(s, b, src):
                dve.wait_ge(xhi_ready, 4 * s["n_xt"] + b + 1)
                return src

            def copy_t(base, b, scale=1.0, dst=None):
                dve.wait_ge(qk_tr, base + b + 1)
                d = dst if dst is not None else arena[:, b * BANK:(b + 1) * BANK]
                if scale == 1.0:
                    nc.vector.tensor_copy(d, ps[:, b % 4, :]).then_inc(qk_dve, 1)
                else:
                    nc.vector.tensor_scalar(d, ps[:, b % 4, :], scale, None, ALU.mult).then_inc(qk_dve, 1)

            def mixed_lo(s, b):
                dve.wait_ge(xhi_ready, 4 * s["n_xt"] + b + 1)
                nc.vector.tensor_tensor(xlo[:, 2 * b:2 * b + 2, :], ps[:, b, :].rearrange("p (k n) -> p k n", k=2),
                                        xhi[:, 2 * b:2 * b + 2, :].bitcast(F32), ALU.subtract).then_inc(xlo_ready, 1)

            def mix_ab(s):
                dve.wait_ge(bias_sem, 16)
                step(nc.vector.memset(BIAS[0:64, :, 0:64], FAR))
                dve.wait_ge(lin_evac, s["n_lin"] - 10 + 3)
                step(nc.vector.tensor_scalar(wsc[:], proj[:, :, C_WI:C_WI + 8], 8.0 ** -0.5, None, ALU.mult))
                for b in range(1, 9, 2):
                    copy_t(0, b)
                for h in range(8):
                    dve.wait_ge(ix_relu, h + 1)
                    for t, (a, b) in enumerate(((256, 384), (0, 256))):
                        if h == 0:
                            ins = nc.vector.tensor_scalar(IXS[:, a:b], REL[0][:, a:b], wsc[:, t, 0:1], None, ALU.mult)
                        else:
                            ins = nc.vector.scalar_tensor_tensor(out=IXS[:, a:b], in0=REL[h % 2][:, a:b],
                                                                 scalar=wsc[:, t, h:h + 1], in1=IXS[:, a:b],
                                                                 op0=ALU.mult, op1=ALU.add)
                        if t == 0:
                            ins.then_inc(dve_step, 1)
                            step.n += 1
                    ins.then_inc(ix_acc, 1)
                    dve.wait_ge(dve_step, step.n)
                    dve.wait_ge(ix_acc, h + 1)
                step(nc.vector.memset(IXS[0:64, 192:256], FAR))
                step(nc.vector.memset(IXS[0:64, 320:384], FAR))
                for r in range(TOPK // 8):
                    for t, (a, b) in enumerate(((256, 384), (0, 256))):
                        ins = nc.vector.max(top8[:, t, :], IXS[:, a:b])
                        ins.then_inc(dve_step, 1)
                        step.n += 1
                    for t, (a, b) in enumerate(((256, 384), (0, 256))):
                        dve.wait_ge(dve_step, step.n - 1 + t if t == 0 else step.n - 1)
                        nc.vector.match_replace(IXS[:, a:b], top8[:, t, :], IXS[:, a:b], TAKEN).then_inc(dve_step, 1)
                        step.n += 1
                    dve.wait_ge(dve_step, step.n)
                step(nc.vector.tensor_scalar(MSK, IXS, TAKEN, 1.0, ALU.is_equal, ALU.subtract))
                step(nc.vector.tensor_scalar(MSK, MSK, -FAR, None, ALU.mult))
                dve.wait_ge(sig_den, 1)
                g = proj[:, :, C_GA:C_GA + 2 * D]
                step(nc.vector.reciprocal(g, g))

                def unit(u):
                    dve.wait_ge(score_ready, u + 1)
                    if u >= 2:
                        dve.wait_ge(ptr_ready, u - 1)
                    bank = ps[:, 4 + u % 2, :]
                    if u < 8:
                        step(nc.vector.scalar_tensor_tensor(out=SC[u % 2][:, 0:256], in0=bank[:, 0:256], scalar=0.125,
                                                            in1=BIAS[:, u, 255::-1], op0=ALU.mult, op1=ALU.add))
                        nc.vector.scalar_tensor_tensor(out=SC[u % 2][:, 256:384], in0=bank[:, 256:384], scalar=0.125,
                                                       in1=BIAS[:, u, 127::-1], op0=ALU.mult, op1=ALU.add
                                                       ).then_inc(biased, 1)
                    else:
                        nc.vector.scalar_tensor_tensor(out=SC[u % 2], in0=bank[:, 0:SPAN], scalar=0.125, in1=MSK,
                                                       op0=ALU.mult, op1=ALU.add).then_inc(biased, 1)
                    dve.wait_ge(biased, u + 1)
                    nc.vector.reduce_max(unit_stat[:, 0, u % 2, 0:1], SC[u % 2][:, 256:384], AX_X)
                    step(nc.vector.reduce_max(unit_stat[:, 0, u % 2, 1:2], SC[u % 2][:, 0:256], AX_X))
                    nc.vector.tensor_scalar(unit_stat[:, 1, u % 2, :], unit_stat[:, 0, u % 2, :], -1.0, None, ALU.mult
                                            ).then_inc(nmax_ready, 1)

                for u in range(18):
                    if u < 16:
                        unit(u)
                    if 1 <= u < 17:
                        dve.wait_ge(p_exp, u)
                        nc.vector.reciprocal(unit_stat[:, 3, (u - 1) % 2, :], unit_stat[:, 2, (u - 1) % 2, :]
                                             ).then_inc(rden_ready, 1)
                    if u >= 2 and (u - 2) % 4 == 3:
                        mixed_lo(s, (u - 2) // 4)

            def branch(s):
                sa, sbr = proj[:, :, C_GA:C_GA + D], proj[:, :, C_GB:C_GB + D]
                dve.wait_ge(br_ready, 1)
                for t in range(NT):
                    step(nc.vector.tensor_tensor(Y[:, t, :], acc_tile(t), sa[:, t, :], ALU.mult))
                dve.wait_ge(br_ready, 2)
                for t in range(NT):
                    pb = ps[:, 4 + 2 * t:6 + 2 * t, :].rearrange("p b n -> p (b n)")
                    step(nc.vector.tensor_tensor(sbr[:, t, :], pb, sbr[:, t, :], ALU.mult))
                    nc.vector.tensor_tensor(Y[:, t, :], Y[:, t, :], sbr[:, t, :], ALU.add).then_inc(y_ready, 1)

            def mix_sb(s):
                base = s["n_qk"]
                for b in range(1, 8, 2):
                    copy_t(base, b, scale=0.125 if b < 4 else 1.0)
                u0 = 16 * s["n_sb"]
                for u in range(18):
                    if u < 16:
                        dve.wait_ge(l_ready, u0 + u + 1)
                        if u >= 4:
                            dve.wait_ge(suf_ready, u0 + u - 3)
                        z = ps[:, 4 + u % 2, 0:SPAN]
                        nc.vector.scalar_tensor_tensor(out=SN[u % 4], in0=z, scalar=0.0, in1=SA[u % 4],
                                                       op0=ALU.max, op1=ALU.add).then_inc(sp_ready, 1)
                        nc.vector.scalar_tensor_tensor(out=SL[u % 4], in0=z, scalar=0.0, in1=SA[u % 4],
                                                       op0=ALU.min, op1=ALU.subtract).then_inc(lb_ready, 1)
                    v = u - 1
                    if 0 <= v < 16:
                        dve.wait_ge(suf_ready, u0 + v + 1)
                        dve.wait_ge(lb_ready, u0 + v + 1)
                        if v >= 4:
                            dve.wait_ge(sbpv_ready, u0 + v - 3)
                        nc.vector.tensor_tensor(SW[v % 4], SL[v % 4], ps[:, 6 + v % 2, 0:SPAN], ALU.subtract
                                                ).then_inc(arg_ready, 1)
                    if v >= 3 and (v - 3) % 4 == 3 and u < 18:
                        mixed_lo(s, (v - 3) // 4 - 0) if (v - 3) // 4 < 3 else None
                mixed_lo(s, 3)

            def mix_conv(s):
                base = s["n_qk"]
                dve.wait_ge(lin_evac, s["n_lin"])
                nc.vector.tensor_tensor(proj[:, 0, D:2 * D], proj[:, 0, D:2 * D], proj[:, 0, 2 * D:3 * D], ALU.mult
                                        ).then_inc(cu_dve, 1)
                step(nc.vector.memset(HT[:, :, 0:2], 0.0))
                for b in range(1, 8, 2):
                    if b < 4:
                        copy_t(base, b, dst=BT[:, 2 * b:2 * b + 2, :].rearrange("p k n -> p (k n)"))
                    else:
                        dve.wait_ge(qk_tr, base + b + 1)
                        nc.vector.tensor_copy(HT[:, 2 * b - 8:2 * b - 6, 2:258],
                                              ps[:, b % 4, :].rearrange("p (k n) -> p k n", k=2)).then_inc(qk_dve, 1)
                dve.wait_ge(qk_act, s["n_qka"] + 4)
                for k in range(KT):
                    dve.wait_ge(tap0_ready, k + 1)
                    for j in (1, 2):
                        step(nc.vector.scalar_tensor_tensor(out=AC[:, k, :], in0=HT[:, k, j:j + 256], scalar=cw[:, k, j:j + 1],
                                                            in1=AC[:, k, :], op0=ALU.mult, op1=ALU.add))
                    nc.vector.tensor_tensor(AC[:, k, :], AC[:, k, :], BT[:, k, :], ALU.mult).then_inc(conv_ready, 1)
                for b in range(4):
                    dve.wait_ge(xhi_ready, 4 * s["n_xt"] + b + 1)
                    nc.vector.tensor_tensor(xlo[:, 2 * b:2 * b + 2, :], AC[:, 2 * b:2 * b + 2, :],
                                            xhi[:, 2 * b:2 * b + 2, :].bitcast(F32), ALU.subtract).then_inc(xlo_ready, 1)

            def mix_gla(s):
                base = s["n_qk"]
                for b in range(1, 4, 2):
                    copy_t(base, b, scale=128.0 ** -0.5 if b < 2 else 1.0, dst=GQK[:, b * BANK:(b + 1) * BANK])
                for j in range(4):
                    dve.wait_ge(gate_ps, j // 2 + 1)
                    ins = nc.vector.tensor_scalar(GC[:, j * 256:(j + 1) * 256], ps[:, 5 + j // 2, (j % 2) * 256:(j % 2 + 1) * 256],
                                                  bgate[:, j:j + 1], None, ALU.add)
                    if j < 3:
                        step(ins)
                ins.then_inc(gz_ready, 1)
                dve.wait_ge(gz_ready, 1)
                step(nc.vector.memset(GQX, 1.0))
                step(nc.vector.memset(GQX.rearrange("p (c n) -> p c n", n=64)[:, :, 0:1], 0.0))
                dve.wait_ge(gl_ready, 1)
                step(nc.vector.scalar_tensor_tensor(out=GC, in0=GC, scalar=0.0, in1=GL, op0=ALU.min, op1=ALU.subtract))
                step(nc.vector.tensor_tensor_scan(GL, GQX, GC, 0.0, ALU.mult, ALU.add))
                nc.vector.tensor_scalar(GC, GL, 1.0 / 16.0, None, ALU.mult).then_inc(cum_ready, 1)
                dve.wait_ge(cum_ready, 1)
                c16 = GC.rearrange("p (b n) -> p b n", n=16)
                c64 = GC.rearrange("p (c n) -> p c n", n=64)
                nc.vector.tensor_tensor(GQX.rearrange("p (b n) -> p b n", n=16), c16, c16[:, :, 7:8].to_broadcast([P, 64, 16]),
                                        ALU.subtract).then_inc(gdiff_ready, 1)
                for a in range(4):
                    w = 16 * (a + 1)
                    nc.vector.tensor_tensor(GK[a].rearrange("p (c n) -> p c n", n=w),
                                            c64[:, :, 16 * a + 7:16 * a + 8].to_broadcast([P, 16, w]), c64[:, :, 0:w],
                                            ALU.subtract).then_inc(gdiff_ready, 1)
                nc.vector.tensor_tensor(GKS.rearrange("p (c n) -> p c n", n=64), c64[:, :, 63:64].to_broadcast([P, 16, 64]), c64,
                                        ALU.subtract).then_inc(gdiff_ready, 1)
                nc.vector.tensor_copy(EL.rearrange("p (c n) -> p c n", n=1), c64[:, :, 63:64]).then_inc(gdiff_ready, 1)
                dve.wait_ge(qk_act, s["n_qka"] + 2)
                dve.wait_ge(gx_ready, 2)
                nc.vector.tensor_tensor(GQX, GQX, GQK[:, 0:1024], ALU.mult).then_inc(qk_scaled, 1)
                kt64 = GQK[:, 1024:2048].rearrange("p (c n) -> p c n", n=64)
                for a in range(4):
                    w = 16 * (a + 1)
                    dve.wait_ge(gx_ready, 3 + a)
                    g = GK[a].rearrange("p (c n) -> p c n", n=w)
                    nc.vector.tensor_tensor(g, g, kt64[:, :, 0:w], ALU.mult).then_inc(qk_scaled, 1)
                step(nc.vector.memset(GS, 0.0))
                dve.wait_ge(swish_den, 1)
                e = proj[:, :, 0:D]
                step(nc.vector.reciprocal(e, e))
                step(nc.vector.tensor_tensor(e, e, proj[:, :, 2 * D:3 * D], ALU.mult))
                dve.wait_ge(gs_ready, 1)
                for half in (0, 64):
                    for a in range(4):
                        w = 16 * (a + 1)
                        o = GS[half:half + w, :].rearrange("p (g n) -> p g n", n=64)[:, :, 16 * a:16 * a + 16]
                        i0 = ps[half:half + w, 4, :].rearrange("p (g n) -> p g n", n=64)[:, :, 16 * a:16 * a + 16]
                        m = const[half:half + w, K_LE + 16 * a:K_LE + 16 * a + 16].unsqueeze(1).to_broadcast([w, 8, 16])
                        ins = nc.vector.tensor_tensor(o, i0, m, ALU.mult)
                        if not (half == 64 and a == 3):
                            step(ins)
                ins.then_inc(gs_sb, 1)
                for n in range(3):
                    dve.wait_ge(upd_ready, n + 1)
                    if n == 0:
                        nc.vector.tensor_copy(GST, ps[:, 6:8, :].rearrange("p b n -> p (b n)")).then_inc(state_ready, 1)
                    else:
                        dve.wait_ge(gx_ready, 8)
                        for h in range(4):
                            ins = nc.vector.scalar_tensor_tensor(
                                out=GST[:, h * 256:(h + 1) * 256], in0=GST[:, h * 256:(h + 1) * 256],
                                scalar=EL[:, 4 * h + n:4 * h + n + 1],
                                in1=ps[:, 6 + h // 2, (h % 2) * 256:(h % 2 + 1) * 256], op0=ALU.mult, op1=ALU.add)
                            if h < 3:
                                step(ins)
                        ins.then_inc(state_ready, 1)
                    dve.wait_ge(state_ready, n + 1)
                row_stat(s, 256, cols=8)
                q = s["n_gain"]
                for t in range(NT):
                    for h in range(4):
                        ins = nc.vector.scalar_tensor_tensor(
                            out=Y[:, t, h * 256:(h + 1) * 256], in0=acc_tile(t)[:, h * 256:(h + 1) * 256],
                            scalar=stat[:, 7, 4 * t + h:4 * t + h + 1], in1=gain[:, q % 2, h * 256:(h + 1) * 256],
                            op0=ALU.mult, op1=ALU.mult)
                        if not (t == 1 and h == 3):
                            step(ins)
                ins.then_inc(gain_used, 1)
                dve.wait_ge(gain_used, q + 1)
                for t in range(NT):
                    nc.vector.tensor_tensor(Y[:, t, :], Y[:, t, :], e[:, t, :], ALU.mult).then_inc(y_ready, 1)

            for index, s in enumerate(STAGES):
                kind = s["kind"]
                q = s["n_gain"]
                if kind == "norm":
                    if s["n_x"] == 0:
                        dve.wait_ge(x_in_sem, 16)
                    else:
                        dve.wait_ge(x_ready, NT * s["n_x"])
                    step(nc.vector.scalar_tensor_tensor(out=Y[:, 1, :], in0=x[:, 1, :], scalar=1.0, in1=x[:, 1, :],
                                                        op0=ALU.mult, op1=ALU.mult, accum_out=stat[:, 0, 1:2]))
                    row_stat(s, D)
                    dst, done = (Y, y_ready) if s["to"] == "y" else (x, x_ready)
                    for t in range(NT):
                        ins = nc.vector.scalar_tensor_tensor(out=dst[:, t, :], in0=x[:, t, :], scalar=stat[:, 7, t:t + 1],
                                                             in1=gain[:, q % 2, :], op0=ALU.mult, op1=ALU.mult)
                        ins.then_inc(done, 1)
                    dve.wait_ge(done, NT * (s["n_y"] if s["to"] == "y" else s["n_x"]) + NT)
                    dve.sem_inc(gain_used, 1)
                elif kind == "addnorm":
                    row_stat(s, D)
                    for t in range(NT):
                        nc.vector.scalar_tensor_tensor(out=Y[:, t, :], in0=acc_tile(t), scalar=stat[:, 7, t:t + 1],
                                                       in1=gain[:, q % 2, :], op0=ALU.mult, op1=ALU.mult
                                                       ).then_inc(dve_step if t == 0 else gain_used, 1)
                    step.n += 1
                    dve.wait_ge(dve_step, step.n)
                    nc.vector.tensor_tensor(x[:, 0, :], x[:, 0, :], Y[:, 0, :], ALU.add).then_inc(x_ready, 1)
                    dve.wait_ge(gain_used, q + 1)
                    nc.vector.tensor_tensor(x[:, 1, :], x[:, 1, :], Y[:, 1, :], ALU.add).then_inc(x_ready, 1)
                elif kind == "add":
                    dve.wait_ge(acc_ready, s["n_acc"])
                    for t in range(NT):
                        nc.vector.scalar_tensor_tensor(out=x[:, t, :], in0=acc_tile(t), scalar=s["scale"], in1=x[:, t, :],
                                                       op0=ALU.mult, op1=ALU.add).then_inc(x_ready, 1)
                elif kind == "trans":
                    for b in range(4):
                        t, half = b // 2, b % 2
                        dve.wait_ge(xhi_ready, 4 * s["n_xt"] + b + 1)
                        part = (slice(None), slice(4 * half, 4 * half + 4), slice(t * P, (t + 1) * P))
                        nc.vector.tensor_tensor(xlo[part], ps[:, b, :].rearrange("p (k n) -> p k n", k=4),
                                                xhi[part].bitcast(F32), ALU.subtract).then_inc(xlo_ready, 1)
                elif kind == "gated":
                    ffn(index, s, FF1_ITERS, True)
                elif kind == "squared":
                    ffn(index, s, FF2_ITERS, False)
                elif kind == "lin":
                    lin(index, s)
                elif kind in ("out", "branch"):
                    if "dve" not in s.get("early", ()):
                        split_next([0, 1])
                    split_next([2, 3])
                    split_early(index)
                    if kind == "branch":
                        branch(s)
                elif kind == "mix_ab":
                    mix_ab(s)
                elif kind == "mix_sb":
                    mix_sb(s)
                elif kind == "mix_conv":
                    mix_conv(s)
                elif kind == "mix_gla":
                    mix_gla(s)

        @block.gpsimd
        def _(pool):
            step = Steps(pool, pool_step)
            line = bass.AP(tensor=bias_line.tensor, offset=0, ap=[[1, P], [383, 8], [1, 256]])
            pool.dma_start(BIAS, line).then_inc(bias_sem, 16)
            pool.wait_ge(const_sem, 16)

            def squared(s):
                up0 = s["n_up"]

                def square(i):
                    pool.wait_ge(relu_ready, i + (s["n_sq"] + 1))
                    if not isinstance(i, int) or i >= 1:
                        pool.wait_ge(ht_ready, i + up0)
                    nc.gpsimd.tensor_tensor(H[:], R[:], R[:], ALU.mult).then_inc(h_ready, 1)

                square(0)
                with pool.Fori(1, FF2_ITERS) as i:
                    square(i)

            def gated(s):
                ones = const[:, K_ONES:K_ONES + 1].unsqueeze(1).to_broadcast([P, NT, FF1_STEP])

                def den(i):
                    pool.wait_ge(gexp_ready, i + (s["n_gt"] + 1))
                    nc.gpsimd.tensor_tensor(EG[:], EG[:], ones, ALU.add).then_inc(gden_ready, 1)

                den(0)
                with pool.Fori(1, FF1_ITERS) as i:
                    den(i)

            def mix_ab(s):
                pool.wait_ge(lin_evac, s["n_lin"] - 10 + 3)
                for t in range(NT):
                    v = proj[:, t, 0:ROPE_HEADS * 64].rearrange("p (h e) -> p h e", e=64)
                    cos = const[:, K_COS + 16 * t:K_COS + 16 * t + 16].unsqueeze(1).to_broadcast([P, ROPE_HEADS, 16])
                    step(nc.gpsimd.tensor_tensor(ROPE_A, v[:, :, 0:16], cos, ALU.mult))
                    for half in (0, 8):
                        sin = const[:, K_SIN + 16 * t + half:K_SIN + 16 * t + half + 8].unsqueeze(1).to_broadcast([P, ROPE_HEADS, 8])
                        step(nc.gpsimd.tensor_tensor(ROPE_B[:, :, half:half + 8], v[:, :, 8 - half:16 - half], sin, ALU.mult))
                    nc.gpsimd.tensor_tensor(v[:, :, 0:16], ROPE_A, ROPE_B, ALU.add).then_inc(rope_done, 1)
                    pool.wait_ge(rope_done, t + 1)
                pool.wait_ge(sig_exp, 1)
                g = proj[:, :, C_GA:C_GA + 2 * D]
                nc.gpsimd.tensor_scalar(g, g, 1.0, None, ALU.add).then_inc(sig_den, 1)
                for u in range(16):
                    pool.wait_ge(rden_ready, u + 1)
                    for t, (a, b) in enumerate(((256, 384), (0, 256))):
                        nc.gpsimd.tensor_scalar(SC[u % 2][:, a:b], SC[u % 2][:, a:b], unit_stat[:, 3, u % 2, t:t + 1], None,
                                                ALU.mult).then_inc(p_ready, 1)

            def mix_sb(s):
                u0 = 16 * s["n_sb"]
                causal = const[:, K_LT:K_LT + P].unsqueeze(1).to_broadcast([P, 2, P])

                def diagonal(buf):
                    return buf.rearrange("p (b n) -> p b n", n=P)[:, 0:3:2, :]

                for u in range(18):
                    if u < 16:
                        pool.wait_ge(sp_ready, u0 + u + 1)
                        nc.gpsimd.tensor_tensor(diagonal(SN[u % 4]), diagonal(SN[u % 4]), causal, ALU.mult).then_inc(spm_ready, 1)
                    v = u - 2
                    if v >= 0:
                        pool.wait_ge(w_exp, u0 + v + 1)
                        nc.gpsimd.tensor_tensor(diagonal(SW[v % 4]), diagonal(SW[v % 4]), causal, ALU.mult).then_inc(w_ready, 1)

            def mix_gla(s):
                pool.wait_ge(swish_exp, 1)
                e = proj[:, :, 0:D]
                nc.gpsimd.tensor_scalar(e, e, 1.0, None, ALU.add).then_inc(swish_den, 1)
                pool.wait_ge(qk_act, s["n_qka"] + 2)
                pool.wait_ge(qk_dve, s["n_qkd"] + 2)
                pool.wait_ge(gx_ready, 1)
                nc.gpsimd.tensor_tensor(GQI, GQI, GQK[:, 0:1024], ALU.mult).then_inc(qk_pool, 1)
                pool.wait_ge(gx_ready, 7)
                nc.gpsimd.tensor_tensor(GKS, GKS, GQK[:, 1024:2048], ALU.mult).then_inc(qk_pool, 1)

            for s in STAGES:
                kind = s["kind"]
                if kind == "gated":
                    gated(s)
                elif kind == "squared":
                    squared(s)
                elif kind == "mix_ab":
                    mix_ab(s)
                elif kind == "mix_sb":
                    mix_sb(s)
                elif kind == "mix_conv":
                    pool.wait_ge(lin_evac, s["n_lin"])
                    nc.gpsimd.tensor_tensor(proj[:, 1, D:2 * D], proj[:, 1, D:2 * D], proj[:, 1, 2 * D:3 * D], ALU.mult
                                            ).then_inc(cu_pool, 1)
                elif kind == "mix_gla":
                    mix_gla(s)

        @block.tensor
        def _(pe):
            slots = Slots()
            pe.wait_ge(const_sem, 16)

            def split_mm(out_ap, a_hi, a_lo, w_slot, panel, first, last):
                wh = whi[w_slot][:, panel * BANK:(panel + 1) * BANK]
                wl = wlo[w_slot][:, panel * BANK:(panel + 1) * BANK]
                nc.tensor.matmul(out_ap, a_hi, wh, start=first, stop=False)
                nc.tensor.matmul(out_ap, a_hi, wl, start=False, stop=False)
                return nc.tensor.matmul(out_ap, a_lo, wh, start=False, stop=last)

            def job(banks, slot_ids, n):
                for j, s in enumerate(slot_ids):
                    pe.wait_ge(lo_ready[s], n[s] + 1)
                    for kk in range(PANELS):
                        k = j * PANELS + kk
                        for t in range(NT):
                            ins = split_mm(ps[:, banks[t], :], xhi[:, k, t * P:(t + 1) * P], xlo[:, k, t * P:(t + 1) * P],
                                           s, kk, k == 0, k == KT - 1)
                    if j == 0:
                        ins.then_inc(w_used[s], 1)
                return ins

            def wide(slot_ids, n, a_hi, a_lo, kt, first, last, bank0=0):
                for j, s in enumerate(slot_ids):
                    pe.wait_ge(lo_ready[s], n[s] + 1)
                    for kk in range(2):
                        k = 2 * j + kk
                        for t in range(NT):
                            for c in range(2):
                                ins = split_mm(ps[:, bank0 + 2 * t + c, :], a_hi(t, k), a_lo(t, k), s, 2 * kk + c,
                                               first and k == 0, last and k == kt - 1)
                    ins.then_inc(w_used[s], 1)

            def done_mark(sem_done, n_wait, ins_sem):
                pass

            def ffn(s, iters, gated):
                dslots = [2] if gated else [2, 3]
                up0 = s["n_up"]
                kt = 2 if gated else 4

                def up(i, n):
                    job((4, 5), (0, 1), n).then_inc(w_used[1], 1)
                    pe.wait_ge(w_used[1], n[1] + 1)
                    pe.sem_inc(up_ready, 1)

                def down(i, n, first, last):
                    pe.wait_ge(hlo_ready, i + (up0 + 1))
                    wide(dslots, n, lambda t, k: hhi[:, t, k, :], lambda t, k: hlo[:, t, k, :], kt, first, last)

                def turn(i):
                    pe.wait_ge(h_ready, i + (up0 + 1))
                    for t in range(NT):
                        for k in range(kt):
                            ins = nc.tensor.transpose(ps[:, 6 + t, k * P:(k + 1) * P], H[:, t, k * P:(k + 1) * P], ident)
                    ins.then_inc(ht_ready, 1)

                ids = [0, 1] + dslots
                pe.wait_ge(xlo_ready, 4 * s["n_xt"])
                up(0, {q: slots.take(q) for q in (0, 1)})
                turn(0)
                n = {q: slots.take(q) for q in ids}
                up(1, n)
                down(0, n, True, False)
                turn(1)
                base = list(slots.n)
                with pe.Fori(2, iters) as i:
                    n = {q: (i - 2) + base[q] for q in ids}
                    up(i, n)
                    down(i - 1, n, False, False)
                    turn(i)
                for q in ids:
                    slots.n[q] += iters - 2
                n = {q: slots.take(q) for q in dslots}
                down(iters - 1, n, False, True)
                pe.wait_ge(w_used[dslots[-1]], n[dslots[-1]] + 1)
                pe.sem_inc(acc_ready, 1)

            def lin(s):
                base = s["n_lin"]
                pe.wait_ge(xlo_ready, 4 * s["n_xt"])

                def two(d, n, first):
                    for c in range(2):
                        if not first:
                            pe.wait_ge(lin_evac, d * 2 + (base + c - 1))
                        ids = (0, 1) if c == 0 else (2, 3)
                        job((4 + 2 * c, 5 + 2 * c), ids, n).then_inc(w_used[ids[1]], 1)
                        pe.wait_ge(w_used[ids[1]], n[ids[1]] + 1)
                        pe.sem_inc(lin_ready, 1)

                two(0, {q: slots.take(q) for q in range(4)}, True)
                n0 = list(slots.n)
                with pe.Fori(1, s["doubles"]) as d:
                    two(d, {q: (d - 1) + n0[q] for q in range(4)}, False)
                for q in range(4):
                    slots.n[q] += s["doubles"] - 1

            def out_layer(s):
                pe.wait_ge(xlo_ready, 4 * s["n_xt"])
                for c in range(2):
                    ids = (0, 1) if c == 0 else (2, 3)
                    n = {q: slots.take(q) for q in ids}
                    job((c, 2 + c), ids, n).then_inc(w_used[ids[1]], 1)
                pe.wait_ge(w_used[3], n[3] + 1)
                pe.sem_inc(acc_ready, 1)

            def branch(s):
                pe.wait_ge(xlo_ready, 4 * s["n_xt"])
                for c in range(2):
                    ids = (0, 1) if c == 0 else (2, 3)
                    n = {q: slots.take(q) for q in ids}
                    wide(ids, n, lambda t, k: xhi[:, 4 * c + k, t * P:(t + 1) * P],
                         lambda t, k: xlo[:, 4 * c + k, t * P:(t + 1) * P], 4, True, True, bank0=4 * c)
                    pe.wait_ge(w_used[ids[1]], n[ids[1]] + 1)
                    pe.sem_inc(br_ready, 1)

            def turn_y(s):
                for t in range(NT):
                    pe.wait_ge(y_ready, 2 * (s["n_y"] - 1) + t + 1)
                    for half in range(2):
                        for k in range(4):
                            f = (4 * half + k) * P
                            ins = nc.tensor.transpose(ps[:, 2 * t + half, k * P:(k + 1) * P], Y[:, t, f:f + P], ident)
                        ins.then_inc(tr_ready, 1)

            def turn_tiles(s, columns, before=None):
                for b in range(len(columns) // 2):
                    if before is not None:
                        before(b)
                    if b >= 4:
                        if b % 2 == 0:
                            pe.wait_ge(qk_act, s["n_qka"] + (b - 4) // 2 + 1)
                        else:
                            pe.wait_ge(qk_dve, s["n_qkd"] + (b - 4) // 2 + 1)
                    for j in range(2):
                        for t in range(NT):
                            c = columns[2 * b + j]
                            ins = nc.tensor.transpose(ps[:, b % 4, j * 256 + t * P:j * 256 + (t + 1) * P],
                                                      proj[:, t, c:c + P], ident)
                    ins.then_inc(qk_tr, 1)
                nb = len(columns) // 2
                return nb

            def wait_tiles(s, nb):
                pe.wait_ge(qk_act, s["n_qka"] + (nb + 1) // 2)
                pe.wait_ge(qk_dve, s["n_qkd"] + nb // 2)

            def tile_of(i):
                return arena[:, i * 256:(i + 1) * 256]

            def mix_ab(s):
                jobs0 = s["n_lin"] - 10
                columns = [P * j for j in range(10)] + [C_QA + P * j for j in range(8)]

                def before(b):
                    if b == 0:
                        pe.wait_ge(rope_done, NT)
                    if b == 5:
                        pe.wait_ge(lin_evac, jobs0 + 5)

                nb = turn_tiles(s, columns, before)
                wait_tiles(s, nb)

                def scores(bank, q, k, r):
                    qt, kt = tile_of(q)[64 * r:64 * r + 64, :], tile_of(k)[64 * r:64 * r + 64, :]
                    nc.tensor.matmul(ps[:, bank, 0:256], qt[:, P:2 * P], kt, start=True, stop=True)
                    return nc.tensor.matmul(ps[:, bank, 256:384], qt[:, 0:P], kt[:, 0:P], start=True, stop=True)

                pe.wait_ge(lin_evac, s["n_lin"])
                for h in range(8):
                    if h >= 4:
                        pe.wait_ge(ix_relu, h - 3)
                    scores(4 + h % 4, 4 + h // 2, 9, h % 2).then_inc(ix_ready, 1)
                pe.wait_ge(ix_relu, 8)
                for u in range(18):
                    if u < 16:
                        if u >= 2:
                            pe.wait_ge(biased, u - 1)
                        if u < 8:
                            ins = scores(4 + u % 2, 10 + u // 2, 14 + u // 2, u % 2)
                        else:
                            ins = scores(4 + u % 2, (u - 8) // 2, 8, u % 2)
                        ins.then_inc(score_ready, 1)
                    v = u - 1
                    if 0 <= v < 16:
                        pe.wait_ge(p_ready, 2 * v + 2)
                        if v >= 2:
                            pe.wait_ge(pt_ready, v - 1)
                        bank = 6 + v % 2
                        nc.tensor.transpose(ps[:, bank, 0:128], SC[v % 2][:, 256:384], ident)
                        nc.tensor.transpose(ps[:, bank, 128:256], SC[v % 2][:, 0:128], ident)
                        nc.tensor.transpose(ps[:, bank, 256:384], SC[v % 2][:, 128:256], ident).then_inc(ptr_ready, 1)
                    v = u - 2
                    if v >= 0:
                        pe.wait_ge(pt_ready, v + 1)
                        c = C_VA + 64 * v if v < 8 else C_VB + 64 * (v % 2)
                        pair, r = v // 2, v % 2
                        o = ps[64 * r:64 * r + 64, pair // 2, (pair % 2) * 256:(pair % 2 + 1) * 256]
                        nc.tensor.matmul(o, proj[:, 0, c:c + 64], PTB[v % 2][:, 0:256], start=True, stop=False)
                        nc.tensor.matmul(o[:, 128:256], proj[:, 1, c:c + 64], PTB[v % 2][:, 256:384], start=False, stop=True
                                         ).then_inc(pv_ready, 1)

            def mix_sb(s):
                u0 = 16 * s["n_sb"]
                pe.wait_ge(lin_evac, s["n_lin"])
                nb = turn_tiles(s, [P * j for j in range(16)])
                wait_tiles(s, nb)
                gt, ones = const[:, K_GT:K_GT + P], const[:, K_ONES:K_ONES + P]
                for u in range(20):
                    if u < 16:
                        if u >= 2:
                            pe.wait_ge(lb_ready, u0 + u - 1)
                        r = u % 2
                        q, k = tile_of(u // 2)[64 * r:64 * r + 64, :], tile_of(8 + u // 2)[64 * r:64 * r + 64, :]
                        nc.tensor.matmul(ps[:, 4 + u % 2, 0:256], k[:, 0:P], q, start=True, stop=True)
                        nc.tensor.matmul(ps[:, 4 + u % 2, 256:384], k[:, P:2 * P], q[:, P:2 * P], start=True, stop=True
                                         ).then_inc(z_ready, 1)
                    v = u - 2
                    if 0 <= v < 16:
                        pe.wait_ge(spm_ready, u0 + v + 1)
                        if v >= 2:
                            pe.wait_ge(arg_ready, u0 + v - 1)
                        bank, n1 = ps[:, 6 + v % 2, :], SN[v % 4]
                        nc.tensor.matmul(bank[:, 256:384], gt, n1[:, 256:384], start=True, stop=True)
                        nc.tensor.matmul(bank[:, 0:256], gt, n1[:, 0:256], start=True, stop=False)
                        nc.tensor.matmul(bank[:, 128:256], ones, n1[:, 256:384], start=False, stop=True).then_inc(suf_ready, 1)
                    v = u - 4
                    if v >= 0:
                        pe.wait_ge(w_ready, u0 + v + 1)
                        pair, r = v // 2, v % 2
                        c = 2 * D + 64 * v
                        o = ps[64 * r:64 * r + 64, pair // 2, (pair % 2) * 256:(pair % 2 + 1) * 256]
                        nc.tensor.matmul(o, proj[:, 0, c:c + 64], SW[v % 4][:, 0:256], start=True, stop=False)
                        nc.tensor.matmul(o[:, 128:256], proj[:, 1, c:c + 64], SW[v % 4][:, 256:384], start=False, stop=True
                                         ).then_inc(sbpv_ready, 1)

            def mix_conv(s):
                pe.wait_ge(lin_evac, s["n_lin"])

                def before(b):
                    if b == 4:
                        pe.wait_ge(cu_dve, 1)
                        pe.wait_ge(cu_pool, 1)

                turn_tiles(s, [P * j for j in range(16)], before)

            def mix_gla(s):
                pe.wait_ge(lin_evac, s["n_lin"])
                pe.wait_ge(small_sem, 64)
                for k in range(KT):
                    nc.tensor.matmul(ps[0:16, 4, 0:SEQ], wlow[:, k, :], xhi[:, k, :].bitcast(F32), start=(k == 0), stop=False)
                    ins = nc.tensor.matmul(ps[0:16, 4, 0:SEQ], wlow[:, k, :], xlo[:, k, :].bitcast(F32), start=False,
                                           stop=(k == KT - 1))
                ins.then_inc(low_ready, 1)
                turn_tiles(s, [P * j for j in range(8)])
                pe.wait_ge(low_sb, 1)
                for j in range(4):
                    ins = nc.tensor.matmul(ps[:, 5 + j // 2, (j % 2) * 256:(j % 2 + 1) * 256], wup[:, j * P:(j + 1) * P],
                                           LOW[0:16, :], start=True, stop=True)
                    if j % 2 == 1:
                        ins.then_inc(gate_ps, 1)
                pe.wait_ge(qk_scaled, 5)
                for h in range(4):
                    for n in range(4):
                        for a in range(4):
                            w, c = 16 * (a + 1), 4 * h + n
                            half, col = 64 * (n % 2), (2 * h + n // 2) * 64 + 16 * a
                            ins = nc.tensor.matmul(ps[half:half + w, 4, col:col + 16], GK[a][:, c * w:(c + 1) * w],
                                                   GQX[:, c * 64 + 16 * a:c * 64 + 16 * a + 16], start=True, stop=True)
                ins.then_inc(gs_ready, 1)
                pe.wait_ge(qk_pool, 2)
                for h in range(4):
                    for t in range(NT):
                        i = 2 * h + t
                        ins = nc.tensor.transpose(ps[:, 6 + i // 4, (i % 4) * P:(i % 4 + 1) * P],
                                                  GKS[:, i * P:(i + 1) * P], ident)
                        if i % 4 == 3:
                            ins.then_inc(kn_ps, 1)
                wait_tiles(s, 4)
                pe.wait_ge(gs_sb, 1)
                pe.wait_ge(kn_sb, 2)
                for n in range(4):
                    t, half = n // 2, 64 * (n % 2)
                    if n >= 1:
                        pe.wait_ge(state_ready, n)
                    for h in range(4):
                        o = ps[half:half + 64, 2 * t + h // 2, (h % 2) * 256:(h % 2 + 1) * 256]
                        v = proj[half:half + 64, t, D + h * 256:D + (h + 1) * 256]
                        if n >= 1:
                            nc.tensor.matmul(o, GQI[:, (4 * h + n) * 64:(4 * h + n + 1) * 64], GST[:, h * 256:(h + 1) * 256],
                                             start=True, stop=False)
                        ins = nc.tensor.matmul(o, GS[half:half + 64, (2 * h + t) * 64:(2 * h + t + 1) * 64], v,
                                               start=(n == 0), stop=True)
                    if n < 3:
                        for h in range(4):
                            v = proj[half:half + 64, t, D + h * 256:D + (h + 1) * 256]
                            ins = nc.tensor.matmul(ps[:, 6 + h // 2, (h % 2) * 256:(h % 2 + 1) * 256],
                                                   GKN[half:half + 64, (2 * h + t) * P:(2 * h + t + 1) * P], v,
                                                   start=True, stop=True)
                        ins.then_inc(upd_ready, 1)
                ins.then_inc(go_ready, 1)

            for s in STAGES:
                kind = s["kind"]
                if kind == "gated":
                    ffn(s, FF1_ITERS, True)
                elif kind == "squared":
                    ffn(s, FF2_ITERS, False)
                elif kind == "lin":
                    lin(s)
                elif kind == "out":
                    out_layer(s)
                elif kind == "branch":
                    branch(s)
                elif kind == "trans":
                    turn_y(s)
                elif kind == "mix_ab":
                    mix_ab(s)
                elif kind == "mix_sb":
                    mix_sb(s)
                elif kind == "mix_conv":
                    mix_conv(s)
                elif kind == "mix_gla":
                    mix_gla(s)


def tall(w, cols):
    n = w.shape[1] // cols
    return w.reshape(2, PANELS, P, n, cols).transpose(3, 0, 2, 1, 4).reshape(n * 2, P, PANELS * cols)


def flat(w):
    return w.reshape(w.shape[0] // 256, 2, P, D).transpose(0, 2, 1, 3).reshape(-1, P, 2 * D)


def kernel(x, n1_g, ffn1_w_in, ffn1_w_out, n2_g, w_in, rel_bias, w_branch_a, w_branch_b, w_out, n3_g,
           ffn2_w_in, ffn2_w_out, nf_g, norm_gains_2, sb_w_qkv_2, sb_w_o_2, conv_w_in_2, conv_w_2,
           conv_w_out_2, gla_w_in_2, gla_w_gate_up_2, gla_b_gate_2, gla_head_norm_2, gla_w_o_2,
           ffn_w_up_2, ffn_w_down_2):
    import concourse.bacc as _bacc
    from concourse.bass_utils import run_bass_kernel_spmd as _run

    def gated_parts(wi, wo):
        gate, up = wi[:, :FF1], wi[:, FF1:]
        both = np.concatenate([gate.reshape(D, FF1_ITERS, 1, FF1_STEP), up.reshape(D, FF1_ITERS, 1, FF1_STEP)], 2)
        u = tall(both.reshape(D, FF1_ITERS * BANK), BANK).reshape(FF1_ITERS, 2, P, PART)
        d = flat(wo).reshape(FF1_ITERS, 1, P, PART)
        return np.concatenate([u, d], 1).reshape(-1, P, PART)

    def squared_parts(wi, wo):
        u = tall(wi, BANK).reshape(FF2_ITERS, 2, P, PART)
        d = flat(wo).reshape(FF2_ITERS, 2, P, PART)
        return np.concatenate([u, d], 1).reshape(-1, P, PART)

    w = w_in[0]
    qa, ka, va, qb, kb, vb, qi, ki, wi, ga, gb = np.split(
        w, [512, 1024, 1536, 2048, 2176, 2304, 2816, 2880, 2888, 3912], axis=1)
    qb = qb.reshape(D, 2, 4, 64).transpose(0, 2, 1, 3).reshape(D, 512)
    w_mix = np.concatenate([qb, qi, kb, ki, ki, vb, wi, np.zeros((D, C_QA - C_WI - 8), w.dtype),
                            qa, ka, va, ga, gb], axis=1)
    w_b = w_branch_b[0].reshape(2, 4, 64, D).transpose(1, 0, 2, 3).reshape(512, D)

    parts = [gated_parts(ffn1_w_in[0], ffn1_w_out[0]), tall(w_mix, BANK), flat(w_branch_a[0]), flat(w_b),
             tall(w_out[0], BANK), gated_parts(ffn2_w_in[0], ffn2_w_out[0])]
    mixers = [(sb_w_qkv_2[0], sb_w_o_2[0]), (conv_w_in_2[0], conv_w_out_2[0]),
              (gla_w_in_2[0][:, :3072], gla_w_o_2[0]), (sb_w_qkv_2[1], sb_w_o_2[1])]
    gain_list = [n1_g[0], n2_g[0], n3_g[0], nf_g]
    for layer in range(DEPTH2):
        wi_l, wo_l = mixers[layer]
        parts += [tall(wi_l, BANK), tall(wo_l, BANK), squared_parts(ffn_w_up_2[layer], ffn_w_down_2[layer])]
        g = norm_gains_2[layer]
        gain_list += [g[0]] + ([gla_head_norm_2[0].reshape(D)] if layer % 3 == 2 else []) + [g[1], g[2], g[3]]

    rel = rel_bias[0]
    arrays = {
        "x": x[0],
        "w_parts": np.concatenate(parts, 0),
        "gains": np.stack(gain_list),
        "const_in": constants(),
        "bias_line": np.concatenate([rel[:, 1:257], np.repeat(rel[:, 256:257], 127, axis=1)], axis=1),
        "conv_w": conv_w_2[0].reshape(3, KT, P).transpose(2, 1, 0),
        "gla_low": gla_w_in_2[0][:, 3072:].reshape(KT, P, 16).transpose(1, 0, 2),
        "gla_up": gla_w_gate_up_2[0],
        "gla_b": gla_b_gate_2[0].reshape(4, P).transpose(1, 0),
    }
    nc = _bacc.Bacc("TRN2", target_bir_lowering=False, num_devices=1)
    feeds, aps = {}, []
    for name, a in arrays.items():
        a = np.ascontiguousarray(a)
        feeds["in_" + name] = a
        aps.append(nc.dram_tensor("in_" + name, a.shape, mybir.dt.from_np(a.dtype), kind="ExternalInput").ap())
    out = nc.dram_tensor("out_0", (SEQ, D), F32, kind="ExternalOutput").ap()
    build(nc, *aps, out)
    r = _run(nc, [feeds], core_ids=[0])
    return r.results[0]["out_0"].reshape(1, SEQ, D)
```

```python
from contextlib import ExitStack

import numpy as np

import concourse.bass as bass
from concourse import mybir

F32 = mybir.dt.float32
F32R = mybir.dt.float32r
ALU = mybir.AluOpType
ACT = mybir.ActivationFunctionType
AX_X = mybir.AxisListType.X

P = 128
SEQ = 256
NT = SEQ // P
D = 1024
KT = D // P
BANK = 512
PANELS = 4
PART = PANELS * BANK
EPS = 1e-6
FAR = -1.0e30
TAKEN = -3.0e38

FF1 = 2816
FF1_STEP = 256
FF1_ITERS = FF1 // FF1_STEP
FF2 = 4096
FF2_STEP = 512
FF2_ITERS = FF2 // FF2_STEP
DEPTH2 = 4

C_QB, C_QI, C_KB, C_KI, C_VB, C_WI = 0, 512, 1024, 1152, 1280, 1408
C_QA, C_KA, C_VA, C_GA, C_GB = 1536, 2048, 2560, 3072, 4096
PCOLS = 5120
ROPE_HEADS = 20
TOPK = 64
SPAN = 384

K_ID, K_ONES, K_GT, K_LT, K_LE, K_COS, K_SIN, KCOLS = 0, 128, 256, 384, 512, 576, 608, 640

ARENA = 6656
EXP_LN_SET = 6
QK_BANKS = {"mix_ab": 9, "mix_sb": 8, "mix_conv": 8, "mix_gla": 4}


def stage_list():
    st = []
    cnt = {}

    def add(kind, **kw):
        kw["kind"] = kind
        st.append(kw)
        return kw

    add("bound", add=None, final=False, turn=True)
    add("gated"); add("bound", add=0.5, final=False, turn=True)
    add("lin", doubles=5); add("mix_ab"); add("branch"); add("turn"); add("out")
    add("bound", add=1.0, final=False, turn=True)
    add("gated"); add("bound", add=0.5, final=True, turn=True)
    for layer in range(DEPTH2):
        add("lin", doubles=3)
        add(("mix_sb", "mix_conv", "mix_gla")[layer % 3])
        if layer % 3 == 2:
            add("turn")
        add("out"); add("bound", add="rms", final=False, turn=True)
        add("squared"); add("bound", add="rms", final=False, turn=layer < DEPTH2 - 1)
    add("store")

    run = {k: 0 for k in ("gain", "y", "xt", "x", "acc", "lin", "tr", "up", "sq", "gt", "chain",
                          "sb", "qk", "qka", "qkd", "rms")}
    for s in st:
        s.update({"n_" + k: v for k, v in run.items()})
        kind = s["kind"]
        if kind in QK_BANKS:
            run["qk"] += QK_BANKS[kind]
            run["qka"] += (QK_BANKS[kind] + 1) // 2
            run["qkd"] += QK_BANKS[kind] // 2
        if kind == "bound":
            if s["add"] == "rms":
                run["gain"] += 1
                run["chain"] += NT
                run["rms"] += 1
            if s["add"] is not None:
                run["x"] += 1
            if s["final"]:
                run["gain"] += 1
                run["chain"] += 1
                run["x"] += 1
            if s["turn"]:
                run["gain"] += 1
                run["chain"] += 1
        if kind == "turn" or kind == "bound" and s["turn"]:
            run["tr"] += 1
            run["xt"] += 1
        if kind in ("branch", "mix_gla") or kind == "bound" and s["turn"]:
            run["y"] += 1
        if kind in ("mix_ab", "mix_sb", "mix_conv"):
            run["xt"] += 1
        if kind in ("out", "gated", "squared"):
            run["acc"] += 1
        if kind == "lin":
            run["lin"] += 2 * s["doubles"]
        elif kind == "mix_sb":
            run["sb"] += 1
        elif kind == "mix_gla":
            run["gain"] += 1
            run["chain"] += 1
        elif kind == "gated":
            run["up"] += FF1_ITERS
            run["gt"] += FF1_ITERS
        elif kind == "squared":
            run["up"] += FF2_ITERS
            run["sq"] += FF2_ITERS
    for before, s in zip(st, st[1:]):
        if before["kind"] == "turn" or before["kind"] == "bound" and before["turn"]:
            s["turns_here"] = before
    for i, s in enumerate(st):
        s["norms"] = sum(b["kind"] == "bound" and b["turn"] for b in st[:i])
        s["xt"], s["xt_tr"] = s["n_xt"], s["n_tr"]
        s["y"] = s["n_y"] - (s["kind"] == "turn")
    return st, run


def constants():
    c = np.zeros((P, KCOLS), np.float32)
    p = np.arange(P)[:, None]
    f = np.arange(P)[None, :]
    c[:, K_ID:K_ID + P] = p == f
    c[:, K_ONES:K_ONES + P] = 1.0
    c[:, K_GT:K_GT + P] = p > f
    c[:, K_LT:K_LT + P] = p < f
    c[:, K_LE:K_LE + 64] = (p % 64) <= f[:, :64]
    inv = np.power(np.float32(500000.0), -np.arange(0, 16, 2, dtype=np.float32) / np.float32(16)).astype(np.float32)
    ang = (np.arange(SEQ, dtype=np.float32)[:, None] * inv[None, :]).astype(np.float32)
    cos = np.cos(ang).astype(np.float32).reshape(NT, P, 8)
    sin = np.sin(ang).astype(np.float32).reshape(NT, P, 8)
    for t in range(NT):
        c[:, K_COS + 16 * t:K_COS + 16 * t + 16] = np.concatenate([cos[t], cos[t]], 1)
        c[:, K_SIN + 16 * t:K_SIN + 16 * t + 16] = np.concatenate([-sin[t], sin[t]], 1)
    return c


def build(nc, x_in, w_parts, gains, const_in, bias_line, conv_w, gla_low, gla_up, gla_b, out):
    STAGES, TOTAL = stage_list()

    with ExitStack() as ctx:
        def sb(name, shape, dt=F32):
            return ctx.enter_context(nc.sbuf_tensor(name, shape, dt))

        def sem(name):
            return ctx.enter_context(nc.semaphore(name))

        raw = [sb(f"raw{s}", [P, PART]) for s in range(4)]
        whi = [sb(f"whi{s}", [P, PART], F32R) for s in range(4)]
        wlo = [sb(f"wlo{s}", [P, PART], F32R) for s in range(4)]
        x = sb("x", [P, NT, D])
        xhi = sb("xhi", [P, KT, SEQ], F32R)
        xlo = sb("xlo", [P, KT, SEQ], F32R)
        hhi = sb("hhi", [P, NT, 4, P], F32R)
        hlo = sb("hlo", [P, NT, 4, P], F32R)
        proj = sb("proj", [P, NT, PCOLS])
        gain = sb("gain", [P, 2, D])
        const = sb("const", [P, KCOLS])
        cw = sb("cw", [P, KT, 3])
        wlow = sb("wlow", [P, KT, 16])
        wup = sb("wup", [16, 512])
        bgate = sb("bgate", [P, 4])
        stat = sb("stat", [P, 10, 6])
        gstat = sb("gstat", [P, 8, 8])
        wsc = sb("wsc", [P, NT, 8])
        top8 = sb("top8", [P, NT, 8])
        unit_stat = sb("unit_stat", [P, 3, 4, 2])
        arena = sb("arena", [P, ARENA])
        ps = ctx.enter_context(nc.psum_tensor("ps", [P, 8, BANK], F32))

        ident = const[:, K_ID:K_ID + P]
        Y = arena[:, 0:2048].rearrange("p (t d) -> p t d", t=NT)
        R = arena[:, 2048:3072].rearrange("p (t f) -> p t f", t=NT)
        H = arena[:, 3072:4096].rearrange("p (t f) -> p t f", t=NT)
        JUNK = [arena[:, 2048:3072], arena[:, 3072:4096]]
        SUM_NORM, FINAL_NORM, ROW_NORM = 0, 2, 4
        RS, NEG_RS = 7, 8
        EG = arena[:, 4096:4608].rearrange("p (t f) -> p t f", t=NT)

        BIAS = arena[:, 4608:6656].rearrange("p (h k) -> p h k", h=8)
        ROPE_A = arena[:, 3584:3904].rearrange("p (h e) -> p h e", e=16)
        ROPE_B = arena[:, 3904:4224].rearrange("p (h e) -> p h e", e=16)
        REL = [proj[:, 0, 0:384], proj[:, 0, 384:768]]
        IXS = proj[:, 0, 768:1152]
        MSK = proj[:, 1, 0:384]
        SC = [proj[:, 0, 1536:1920], proj[:, 0, 1920:2304], proj[:, 1, 384:768], proj[:, 1, 768:1152]]
        PTB = [proj[:, 1, 1536:1920], proj[:, 1, 1920:2304]] + REL
        spare = [arena[:, 4096 + SPAN * i:4096 + SPAN * (i + 1)] for i in range(6)]
        spare += [proj[:, t, 3072 + SPAN * i:3072 + SPAN * (i + 1)] for t in range(NT) for i in range(5)]
        SA, SN, SL, SW = spare[0:4], spare[4:8], spare[8:12], spare[12:16]
        BT = arena[:, 0:2048].rearrange("p (k n) -> p k n", k=KT)
        HT = arena[:, 2048:4112].rearrange("p (k n) -> p k n", k=KT)
        AC = arena[:, 4112:6160].rearrange("p (k n) -> p k n", k=KT)
        GQK = arena[:, 0:2048]
        GC = arena[:, 2048:3072]
        GL = arena[:, 3072:4096]
        GQX = arena[:, 4096:5120]
        GQI = arena[:, 5120:6144]
        LOW = arena[:, 6144:6400]
        LOWN = arena[:, 6416:6448]
        EL = arena[:, 6400:6416]
        GKN, GST = GQK[:, 0:1024], GL
        GK = [proj[:, 0, 3072:3328], proj[:, 0, 3328:3840], proj[:, 0, 3840:4608], proj[:, 1, 3072:4096]]
        GKS = proj[:, 1, 4096:5120]
        GS = proj[:, 0, 4608:5120]

        def acc_tile(t):
            return ps[:, 2 * t:2 * t + 2, :].rearrange("p b n -> p (b n)")

        raw_in = [sem(f"raw_in{s}") for s in range(4)]
        hi_ready = [sem(f"hi_ready{s}") for s in range(4)]
        lo_ready = [sem(f"lo_ready{s}") for s in range(4)]
        w_used = [sem(f"w_used{s}") for s in range(4)]
        x_tile_in = [sem("x_tile_in0"), sem("x_tile_in1")]
        const_sem = sem("const_in")
        small_sem = sem("small_in")
        bias_sem = sem("bias_in")
        gain_in = [sem("gain_in0"), sem("gain_in1")]
        gain_used = sem("gain_used")
        x_ready = sem("x_ready")
        norm_ready = sem("norm_ready")
        bank0_squared = sem("bank0_squared")
        bank1_read = sem("bank1_read")
        sum_ready = sem("sum_ready")
        var_ready = sem("var_ready")
        log_ready = sem("log_ready")
        rs_ready = sem("rs_ready")
        y_ready = sem("y_ready")
        tr_ready = sem("tr_ready")
        xhi_ready = sem("xhi_ready")
        xlo_ready = sem("xlo_ready")
        lin_evac = sem("lin_evac")
        acc_ready = sem("acc_ready")
        relu_ready = sem("relu_ready")
        gexp_ready = sem("gexp_ready")
        glog_ready = sem("glog_ready")
        sig_ready = sem("sig_ready")
        gact_ready = sem("gact_ready")
        h_ready = sem("h_ready")
        ht_ready = sem("ht_ready")
        hhi_ready = sem("hhi_ready")
        hlo_ready = sem("hlo_ready")
        qk_tr = sem("qk_tr")
        qk_act = sem("qk_act")
        qk_dve = sem("qk_dve")
        dve_step = sem("dve_step")
        act_step = sem("act_step")
        pool_step = sem("pool_step")
        rope_done = sem("rope_done")
        ix_ready = sem("ix_ready")
        ix_relu = sem("ix_relu")
        ix_acc = sem("ix_acc")
        branch_gates = sem("branch_gates")
        score_ready = sem("score_ready")
        biased = sem("biased")
        nmax_ready = sem("nmax_ready")
        p_exp = sem("p_exp")
        rden_ready = sem("rden_ready")
        p_ready = sem("p_ready")
        ptr_ready = sem("ptr_ready")
        pt_ready = sem("pt_ready")
        pv_ready = sem("pv_ready")
        br_ready = sem("br_ready")
        z_ready = sem("z_ready")
        l_ready = sem("l_ready")
        sp_ready = sem("sp_ready")
        lb_ready = sem("lb_ready")
        spm_ready = sem("spm_ready")
        suf_ready = sem("suf_ready")
        arg_ready = sem("arg_ready")
        w_exp = sem("w_exp")
        w_ready = sem("w_ready")
        sbpv_ready = sem("sbpv_ready")
        cu_dve = sem("cu_dve")
        cu_pool = sem("cu_pool")
        tap0_ready = sem("tap0_ready")
        conv_ready = sem("conv_ready")
        low_ready = sem("low_ready")
        low_sb = sem("low_sb")
        gate_ps = sem("gate_ps")
        gz_ready = sem("gz_ready")
        gl_ready = sem("gl_ready")
        cum_ready = sem("cum_ready")
        gdiff_ready = sem("gdiff_ready")
        gx_ready = sem("gx_ready")
        qk_scaled = sem("qk_scaled")
        qk_pool = sem("qk_pool")
        gs_ready = sem("gs_ready")
        gs_sb = sem("gs_sb")
        kn_ps = sem("kn_ps")
        kn_sb = sem("kn_sb")
        upd_ready = sem("upd_ready")
        state_ready = sem("state_ready")
        go_ready = sem("go_ready")
        swish_ready = sem("swish_ready")
        out_done = sem("out_done")

        GAINS = TOTAL["gain"]

        def more_weights(index):
            return any(s["kind"] in ("gated", "squared", "lin", "out", "branch") for s in STAGES[index + 1:])

        class Slots:
            def __init__(self):
                self.n = [0, 0, 0, 0]

            def take(self, s):
                self.n[s] += 1
                return self.n[s] - 1

        class Steps:
            def __init__(self, eng, s):
                self.eng, self.s, self.n = eng, s, 0

            def __call__(self, ins):
                self.n += 1
                ins.then_inc(self.s, 1)
                self.eng.wait_ge(self.s, self.n)

        block = ctx.enter_context(nc.Block())

        @block.sync
        def _(sp):
            slots = Slots()
            gains_sent = [0]
            state = {"part": 0}

            def load_part(s, part, n):
                if not isinstance(n, int) or n >= 1:
                    sp.wait_ge(lo_ready[s], n)
                sp.dma_start(raw[s][:], w_parts[bass.ds(part, 1), :, :].rearrange("a p n -> (a p) n")
                             ).then_inc(raw_in[s], 16)

            def load_parts(slot_ids):
                for s in slot_ids:
                    load_part(s, state["part"], slots.take(s))
                    state["part"] += 1

            def loop_parts(slot_ids, first, last):
                base, part0 = list(slots.n), state["part"]
                with sp.Fori(first, last) as i:
                    for j, s in enumerate(slot_ids):
                        load_part(s, (i - first) * len(slot_ids) + (part0 + j), (i - first) + base[s])
                for s in slot_ids:
                    slots.n[s] += last - first
                state["part"] += (last - first) * len(slot_ids)

            def load_gains(upto):
                while gains_sent[0] < min(upto, GAINS):
                    q = gains_sent[0]
                    if q >= 2:
                        sp.wait_ge(gain_used, q - 1)
                    sp.dma_start(gain[:, q % 2, :], gains[q:q + 1, :].to_broadcast([P, D])
                                 ).then_inc(gain_in[q % 2], 16)
                    gains_sent[0] += 1

            def load_ffn(down_slots, s, iters):
                load_parts([0, 1])
                load_parts([0, 1] + down_slots)
                load_gains(s["n_gain"] + 2)
                loop_parts([0, 1] + down_slots, 2, iters)
                load_parts(down_slots)

            load_gains(1)
            for s in STAGES:
                kind = s["kind"]
                if kind == "gated":
                    load_ffn([2], s, FF1_ITERS)
                elif kind == "squared":
                    load_ffn([2, 3], s, FF2_ITERS)
                elif kind == "lin":
                    load_parts([0, 1, 2, 3])
                    load_gains(s["n_gain"] + 2)
                    loop_parts([0, 1, 2, 3], 1, s["doubles"])
                elif kind in ("out", "branch"):
                    load_parts([0, 1, 2, 3])
                    load_gains(s["n_gain"] + 2)
                elif kind == "store":
                    sp.wait_ge(x_ready, NT * s["n_x"])
                    for t in range(NT):
                        sp.dma_start(out[t * P:(t + 1) * P, :], x[:, t, :]).then_inc(out_done, 16)
                    sp.wait_ge(out_done, 16 * NT)

        @block.scalar
        def _(act):
            slots = Slots()
            step = Steps(act, act_step)
            nc.scalar.add_instruction(mybir.InstLoadActFuncSet(
                name=nc.get_next_instruction_name(), act_func_set_id=EXP_LN_SET, engine=mybir.EngineType.Activation))

            for t in range(NT):
                act.dma_start(x[:, t, :], x_in[t * P:(t + 1) * P, :]).then_inc(x_tile_in[t], 16)
            act.dma_start(const[:], const_in).then_inc(const_sem, 16)
            for dst, src in ((cw[:], conv_w), (wlow[:], gla_low), (wup[:], gla_up), (bgate[:], gla_b)):
                act.dma_start(dst, src).then_inc(small_sem, 16)

            def split_hi(s, n):
                act.wait_ge(raw_in[s], (n + 1) * 16)
                if not isinstance(n, int) or n >= 1:
                    act.wait_ge(w_used[s], n)
                nc.scalar.activation(whi[s][:], raw[s][:], ACT.Copy).then_inc(hi_ready[s], 1)

            def split_next(ids):
                for s in ids:
                    split_hi(s, slots.take(s))

            def split_early(index):
                if more_weights(index):
                    split_next([0, 1])

            def sigmoid(g):
                step(nc.scalar.activation(g, g, ACT.Exp, scale=-1.0))
                step(nc.scalar.activation(g, g, ACT.Ln, bias=1.0))
                return nc.scalar.activation(g, g, ACT.Exp, scale=-1.0)

            def chain_log(st, c0, c1, chain):
                act.wait_ge(var_ready, chain + 1)
                nc.scalar.activation(st[:, 2, c0:c1], st[:, 1, c0:c1], ACT.Ln).then_inc(log_ready, 1)
                act.wait_ge(log_ready, chain + 1)
                nc.scalar.activation(st[:, 3, c0:c1], st[:, 2, c0:c1], ACT.Exp, scale=-0.5).then_inc(rs_ready, 1)

            def ffn(index, s, iters, gated):
                dslots = [2] if gated else [2, 3]
                up0 = s["n_up"]
                kt = 2 if gated else 4

                def hidden_hi(i):
                    act.wait_ge(ht_ready, i + (up0 + 1))
                    nc.scalar.activation(hhi[:, :, 0:kt, :], ps[:, 6:8, 0:kt * P].rearrange("p t (k n) -> p t k n", k=kt),
                                         ACT.Copy).then_inc(hhi_ready, 1)

                def activate(i, n1):
                    act.wait_ge(w_used[1], n1 + 1)
                    if gated:
                        if not isinstance(i, int) or i >= 1:
                            act.wait_ge(h_ready, i + up0)
                        for t in range(NT):
                            ins = nc.scalar.activation(EG[:, t, :], ps[:, 4 + t, 0:FF1_STEP], ACT.Exp,
                                                       scale=stat[:, NEG_RS, ROW_NORM + t:ROW_NORM + t + 1])
                        ins.then_inc(gexp_ready, 1)
                        act.wait_ge(gexp_ready, i + (s["n_gt"] + 1))
                        nc.scalar.activation(EG[:], EG[:], ACT.Ln, bias=1.0).then_inc(glog_ready, 1)
                        act.wait_ge(glog_ready, i + (s["n_gt"] + 1))
                        nc.scalar.activation(EG[:], EG[:], ACT.Exp, scale=-1.0).then_inc(sig_ready, 1)
                    else:
                        if not isinstance(i, int) or i >= 1:
                            act.wait_ge(h_ready, i + up0)
                        for t in range(NT):
                            ins = nc.scalar.activation(R[:, t, :], ps[:, 4 + t, :], ACT.Relu,
                                                       scale=stat[:, RS, ROW_NORM + t:ROW_NORM + t + 1])
                        ins.then_inc(relu_ready, 1)

                def body(i, n, after):
                    hidden_hi(i - 1)
                    for q in dslots:
                        split_hi(q, n[q])
                    after(0)
                    activate(i, n[1])
                    after(1)

                act.wait_ge(norm_ready, s["norms"])
                split_next([0])
                activate(0, slots.n[1] - 1)
                split_next([1])

                def step_of(i, base):
                    n = {q: (i - 1) + base[q] for q in dslots}
                    n[1] = (i - 1) + (base[1] - 1)
                    body(i, n, lambda q: split_hi(q, (i - 1) + base[q]))

                base = list(slots.n)
                step_of(1, base)
                with act.Fori(2, iters - 1) as i:
                    step_of(i, base)
                for q in [0, 1] + dslots:
                    slots.n[q] += iters - 2
                first_use = slots.n[1] - 1
                following = more_weights(index)
                body(iters - 1, {**{q: slots.take(q) for q in dslots}, 1: first_use},
                     lambda q: split_next([q]) if following else None)
                hidden_hi(iters - 1)
                split_next(dslots)

            def lin(index, s):
                base = s["n_lin"]

                def evac(j, slot, n):
                    act.wait_ge(w_used[slot], n + 1)
                    for t in range(NT):
                        ins = nc.scalar.activation(proj[:, t, bass.ds(j * BANK, BANK)], ps[:, 3 + slot + t, :], ACT.Copy,
                                                   scale=stat[:, RS, ROW_NORM + t:ROW_NORM + t + 1])
                    ins.then_inc(lin_evac, 1)

                act.wait_ge(norm_ready, s["norms"])
                n0 = list(slots.n)
                with act.Fori(0, s["doubles"] - 1) as d:
                    for q in (2, 3):
                        split_hi(q, d + n0[q])
                    evac(d * 2, 1, d + (n0[1] - 1))
                    for q in (0, 1):
                        split_hi(q, d + n0[q])
                    evac(d * 2 + 1, 3, d + n0[3])
                for q in range(4):
                    slots.n[q] += s["doubles"] - 1
                last = 2 * (s["doubles"] - 1)
                split_next([2, 3])
                evac(last, 1, slots.n[1] - 1)
                split_early(index)
                evac(last + 1, 3, slots.n[3] - 1)

            def turned_hi(s, t):
                for half in range(2):
                    b = 2 * t + half
                    act.wait_ge(tr_ready, 4 * s["xt_tr"] + b + 1)
                    nc.scalar.activation(xhi[:, 4 * half:4 * half + 4, t * P:(t + 1) * P],
                                         ps[:, b, :].rearrange("p (k n) -> p k n", k=4), ACT.Copy).then_inc(xhi_ready, 1)

            def squares(src, st, col, ins_sem):
                return nc.scalar.activation(JUNK[col % 2], src, ACT.Square, accum_out=st[:, 0, col:col + 1]).then_inc(ins_sem, 1)

            def bound(s):
                chain = s["n_chain"]
                xs = NT * s["n_x"]
                if s["add"] == "rms":
                    for t in range(NT):
                        act.wait_ge(acc_ready, NT * (s["n_acc"] - 1) + t + 1)
                        nc.scalar.activation(JUNK[t][:, 0:BANK], ps[:, 2 * t, :], ACT.Square,
                                             accum_out=stat[:, 0, SUM_NORM + t:SUM_NORM + t + 1]).then_inc(bank0_squared, 1)
                        act.wait_ge(bank1_read, NT * s["n_rms"] + t + 1)
                        nc.scalar.activation(JUNK[t][:, BANK:D], ps[:, 2 * t + 1, :], ACT.Square,
                                             accum_out=stat[:, 9, SUM_NORM + t:SUM_NORM + t + 1]).then_inc(sum_ready, 1)
                        chain_log(stat, SUM_NORM + t, SUM_NORM + t + 1, chain)
                        chain += 1
                if s["add"] is not None:
                    xs += NT
                if s["final"]:
                    for t in range(NT):
                        act.wait_ge(x_ready, xs - NT + t + 1)
                        if t == 0:
                            step(nc.scalar.activation(JUNK[0], x[:, 0, :], ACT.Square, accum_out=stat[:, 0, FINAL_NORM:FINAL_NORM + 1]))
                        else:
                            squares(x[:, 1, :], stat, FINAL_NORM + 1, sum_ready)
                    chain_log(stat, FINAL_NORM, FINAL_NORM + NT, chain)
                    chain += 1
                    xs += NT
                if s["turn"]:
                    for t in range(NT):
                        turned_hi(s, t)
                        if s["add"] is not None:
                            act.wait_ge(x_ready, xs - NT + t + 1)
                        else:
                            act.wait_ge(x_tile_in[t], 16)
                        if t == 0:
                            step(nc.scalar.activation(JUNK[0], x[:, 0, :], ACT.Square, accum_out=stat[:, 0, ROW_NORM:ROW_NORM + 1]))
                        else:
                            squares(x[:, 1, :], stat, ROW_NORM + 1, sum_ready)
                    chain_log(stat, ROW_NORM, ROW_NORM + NT, chain)

            def copy_t(base, b, scale=1.0, dst=None):
                act.wait_ge(qk_tr, base + b + 1)
                d = dst if dst is not None else arena[:, b * BANK:(b + 1) * BANK]
                return nc.scalar.activation(d, ps[:, b % 4, :], ACT.Copy, scale=scale).then_inc(qk_act, 1)

            def mix_ab(s):
                for b in range(0, 9, 2):
                    copy_t(0, b)
                for h in range(8):
                    act.wait_ge(ix_ready, h + 1)
                    if h >= 2:
                        act.wait_ge(ix_acc, h - 1)
                    nc.scalar.activation(REL[h % 2], ps[:, 4 + h % 4, 0:SPAN], ACT.Relu, scale=0.125).then_inc(ix_relu, 1)

                def exps(u):
                    act.wait_ge(nmax_ready, u + 1)
                    for t, (a, b) in enumerate(((256, 384), (0, 256))):
                        ins = nc.scalar.activation(SC[u % 4][:, a:b], SC[u % 4][:, a:b], ACT.Exp, scale=-1.0,
                                                   bias=unit_stat[:, 0, u % 4, t:t + 1],
                                                   accum_out=unit_stat[:, 1, u % 4, t:t + 1])
                    ins.then_inc(p_exp, 1)

                def pt_copy(u):
                    act.wait_ge(ptr_ready, u + 1)
                    if u >= 4:
                        act.wait_ge(pv_ready, u - 3)
                    nc.scalar.activation(PTB[u % 4], ps[:, 6 + u % 2, 0:SPAN], ACT.Copy).then_inc(pt_ready, 1)

                def o_hi(b):
                    act.wait_ge(pv_ready, 4 * b + 4)
                    nc.scalar.activation(xhi[:, 2 * b:2 * b + 2, :], ps[:, b, :].rearrange("p (k n) -> p k n", k=2),
                                         ACT.Copy).then_inc(xhi_ready, 1)

                act.wait_ge(ix_acc, 8)
                for u in range(19):
                    if u < 16:
                        exps(u)
                    if 2 <= u < 18:
                        pt_copy(u - 2)
                    if u >= 3 and (u - 3) % 4 == 3 and u < 18:
                        o_hi((u - 3) // 4)
                o_hi(3)

            def mix_sb(s):
                r = s["n_sb"]
                base = s["n_qk"]
                for b in range(0, 8, 2):
                    copy_t(base, b, scale=0.125 if b < 4 else 1.0)
                u0 = 16 * r
                for u in range(18):
                    if u < 16:
                        act.wait_ge(z_ready, u0 + u + 1)
                        if u >= 4:
                            act.wait_ge(lb_ready, u0 + u - 3)
                        step(nc.scalar.activation(SA[u % 4], ps[:, 4 + u % 2, 0:SPAN], ACT.Abs))
                        step(nc.scalar.activation(SA[u % 4], SA[u % 4], ACT.Exp, scale=-1.0))
                        nc.scalar.activation(SA[u % 4], SA[u % 4], ACT.Ln, bias=1.0).then_inc(l_ready, 1)
                    v = u - 2
                    if v >= 0:
                        act.wait_ge(arg_ready, u0 + v + 1)
                        nc.scalar.activation(SW[v % 4], SW[v % 4], ACT.Exp).then_inc(w_exp, 1)
                    if v >= 2 and (v - 2) % 4 == 3:
                        sb_o_hi(u0, (v - 2) // 4)
                sb_o_hi(u0, 3)

            def sb_o_hi(u0, b):
                act.wait_ge(sbpv_ready, u0 + 4 * b + 4)
                nc.scalar.activation(xhi[:, 2 * b:2 * b + 2, :], ps[:, b, :].rearrange("p (k n) -> p k n", k=2),
                                     ACT.Copy).then_inc(xhi_ready, 1)

            def mix_conv(s):
                base = s["n_qk"]
                for b in range(0, 8, 2):
                    if b < 4:
                        copy_t(base, b, dst=BT[:, 2 * b:2 * b + 2, :].rearrange("p k n -> p (k n)"))
                    else:
                        act.wait_ge(qk_tr, base + b + 1)
                        nc.scalar.activation(HT[:, 2 * b - 8:2 * b - 6, 2:258], ps[:, b % 4, :].rearrange("p (k n) -> p k n", k=2),
                                             ACT.Copy).then_inc(qk_act, 1)
                act.wait_ge(small_sem, 64)
                for k in range(KT):
                    if k % 4 == 0:
                        act.wait_ge(qk_act, s["n_qka"] + 3 + k // 4)
                        act.wait_ge(qk_dve, s["n_qkd"] + 3 + k // 4)
                    nc.scalar.activation(AC[:, k, :], HT[:, k, 0:256], ACT.Copy, scale=cw[:, k, 0:1]).then_inc(tap0_ready, 1)
                for b in range(4):
                    act.wait_ge(conv_ready, 2 * b + 2)
                    nc.scalar.activation(xhi[:, 2 * b:2 * b + 2, :], AC[:, 2 * b:2 * b + 2, :], ACT.Copy).then_inc(xhi_ready, 1)

            def mix_gla(s):
                base = s["n_qk"]
                act.wait_ge(low_ready, 1)
                for t in range(NT):
                    ins = nc.scalar.activation(LOWN[:, 16 * t:16 * t + 16], ps[:, 4, 16 * t:16 * t + 16], ACT.Copy,
                                               scale=stat[:, RS, ROW_NORM + t:ROW_NORM + t + 1])
                ins.then_inc(low_sb, 1)
                act.wait_ge(low_ready, 2)
                nc.scalar.activation(LOW[0:16, :], ps[0:16, 7, 0:SEQ], ACT.Copy).then_inc(low_sb, 1)
                for b in range(0, 4, 2):
                    copy_t(base, b, scale=128.0 ** -0.5 if b < 2 else 1.0, dst=GQK[:, b * BANK:(b + 1) * BANK])
                act.wait_ge(lin_evac, s["n_lin"])
                act.wait_ge(gz_ready, 1)
                step(nc.scalar.activation(GL, GC, ACT.Abs))
                step(nc.scalar.activation(GL, GL, ACT.Exp, scale=-1.0))
                nc.scalar.activation(GL, GL, ACT.Ln, bias=1.0).then_inc(gl_ready, 1)
                act.wait_ge(cum_ready, 1)
                nc.scalar.activation(GQI, GC, ACT.Exp).then_inc(gx_ready, 1)
                act.wait_ge(gdiff_ready, 1)
                nc.scalar.activation(GQX, GQX, ACT.Exp).then_inc(gx_ready, 1)
                for a in range(4):
                    act.wait_ge(gdiff_ready, 2 + a)
                    nc.scalar.activation(GK[a], GK[a], ACT.Exp).then_inc(gx_ready, 1)
                act.wait_ge(gdiff_ready, 6)
                nc.scalar.activation(GKS, GKS, ACT.Exp).then_inc(gx_ready, 1)
                act.wait_ge(gdiff_ready, 7)
                nc.scalar.activation(EL[:], EL[:], ACT.Exp).then_inc(gx_ready, 1)
                act.wait_ge(qk_tr, base + 4)
                e = proj[:, :, 0:D]
                step(nc.scalar.activation(e, proj[:, :, 2 * D:3 * D], ACT.Exp, scale=-1.0))
                step(nc.scalar.activation(e, e, ACT.Ln, bias=1.0))
                nc.scalar.activation(e, e, ACT.Exp, scale=-1.0).then_inc(swish_ready, 1)
                for b in range(2):
                    act.wait_ge(kn_ps, b + 1)
                    nc.scalar.activation(GKN[:, b * BANK:(b + 1) * BANK], ps[:, 6 + b, :], ACT.Copy).then_inc(kn_sb, 1)
                act.wait_ge(go_ready, 1)
                for t in range(NT):
                    for h in range(4):
                        ins = nc.scalar.activation(GQI[:, 0:256], acc_tile(t)[:, h * 256:(h + 1) * 256], ACT.Square,
                                                   accum_out=gstat[:, 0, 4 * t + h:4 * t + h + 1])
                        if not (t == 1 and h == 3):
                            step(ins)
                ins.then_inc(sum_ready, 1)
                chain_log(gstat, 0, 8, s["n_chain"])

            split_early(-1)
            for index, s in enumerate(STAGES):
                kind = s["kind"]
                if kind == "bound":
                    bound(s)
                elif kind == "turn":
                    for t in range(NT):
                        turned_hi(s, t)
                elif kind == "gated":
                    ffn(index, s, FF1_ITERS, True)
                elif kind == "squared":
                    ffn(index, s, FF2_ITERS, False)
                elif kind == "lin":
                    lin(index, s)
                elif kind == "out":
                    split_next([2, 3])
                    split_early(index)
                elif kind == "branch":
                    split_next([2])
                    sigmoid(proj[:, :, C_GA:C_GA + D]).then_inc(branch_gates, 1)
                    split_next([3])
                    sigmoid(proj[:, :, C_GB:C_GB + D]).then_inc(branch_gates, 1)
                    split_early(index)
                elif kind == "mix_ab":
                    mix_ab(s)
                elif kind == "mix_sb":
                    mix_sb(s)
                elif kind == "mix_conv":
                    mix_conv(s)
                elif kind == "mix_gla":
                    mix_gla(s)

        @block.vector
        def _(dve):
            slots = Slots()
            step = Steps(dve, dve_step)

            def split_lo(s, n):
                dve.wait_ge(hi_ready[s], n + 1)
                nc.vector.tensor_tensor(wlo[s][:], raw[s][:], whi[s][:].bitcast(F32), ALU.subtract).then_inc(lo_ready[s], 1)

            def split_next(ids):
                for s in ids:
                    split_lo(s, slots.take(s))

            def split_early(index):
                if more_weights(index):
                    split_next([0, 1])

            def rsqrt_chain(st, c0, c1, chain, width, halves=False):
                dve.wait_ge(sum_ready, chain + 1)
                if halves:
                    step(nc.vector.tensor_tensor(st[:, 0, c0:c1], st[:, 0, c0:c1], st[:, 9, c0:c1], ALU.add))
                nc.vector.tensor_scalar(st[:, 1, c0:c1], st[:, 0, c0:c1], 1.0 / width, EPS, ALU.mult, ALU.add
                                        ).then_inc(var_ready, 1)
                dve.wait_ge(rs_ready, chain + 1)
                step(nc.vector.tensor_tensor(st[:, 4, c0:c1], st[:, 3, c0:c1], st[:, 3, c0:c1], ALU.mult))
                step(nc.vector.tensor_tensor(st[:, 5, c0:c1], st[:, 4, c0:c1], st[:, 1, c0:c1], ALU.mult))
                step(nc.vector.tensor_scalar(st[:, 6, c0:c1], st[:, 5, c0:c1], -0.5, 1.5, ALU.mult, ALU.add))
                step(nc.vector.tensor_tensor(st[:, RS, c0:c1], st[:, 6, c0:c1], st[:, 3, c0:c1], ALU.mult))

            def wait_gain(q):
                dve.wait_ge(gain_in[q % 2], 16 * (q // 2 + 1))

            def turned_lo(s, t):
                for half in range(2):
                    b = 2 * t + half
                    dve.wait_ge(xhi_ready, 4 * s["xt"] + b + 1)
                    part = (slice(None), slice(4 * half, 4 * half + 4), slice(t * P, (t + 1) * P))
                    nc.vector.tensor_tensor(xlo[part], ps[:, b, :].rearrange("p (k n) -> p k n", k=4),
                                            xhi[part].bitcast(F32), ALU.subtract).then_inc(xlo_ready, 1)

            def bound(s):
                chain, q, xs = s["n_chain"], s["n_gain"], NT * s["n_x"]
                q_turn = q + (s["add"] == "rms") + s["final"]

                def times_gain(t):
                    if t == 0:
                        wait_gain(q_turn)
                    if s["add"] is not None:
                        dve.wait_ge(x_ready, xs + t + 1)
                    else:
                        dve.wait_ge(x_tile_in[t], 16)
                    nc.vector.tensor_tensor(Y[:, t, :], x[:, t, :], gain[:, q_turn % 2, :], ALU.mult).then_inc(y_ready, 1)

                for t in range(NT):
                    if s["add"] is not None:
                        dve.wait_ge(acc_ready, NT * (s["n_acc"] - 1) + t + 1)
                    if s["add"] == "rms":
                        wait_gain(q)
                        nc.vector.tensor_tensor(Y[:, t, BANK:D], ps[:, 2 * t + 1, :], gain[:, q % 2, BANK:D], ALU.mult
                                                ).then_inc(bank1_read, 1)
                        dve.wait_ge(bank0_squared, NT * s["n_rms"] + t + 1)
                        nc.vector.tensor_tensor(Y[:, t, 0:BANK], ps[:, 2 * t, :], gain[:, q % 2, 0:BANK], ALU.mult
                                                ).then_inc(dve_step if t == 0 else gain_used, 1)
                        if t == 0:
                            step.n += 1
                        rsqrt_chain(stat, SUM_NORM + t, SUM_NORM + t + 1, chain, D, halves=True)
                        chain += 1
                        if t == 1:
                            dve.wait_ge(gain_used, q + 1)
                        nc.vector.scalar_tensor_tensor(out=x[:, t, :], in0=Y[:, t, :], scalar=stat[:, RS, SUM_NORM + t:SUM_NORM + t + 1],
                                                       in1=x[:, t, :], op0=ALU.mult, op1=ALU.add).then_inc(x_ready, 1)
                    elif s["add"] is not None:
                        nc.vector.scalar_tensor_tensor(out=x[:, t, :], in0=acc_tile(t), scalar=s["add"], in1=x[:, t, :],
                                                       op0=ALU.mult, op1=ALU.add).then_inc(x_ready, 1)
                    if s["turn"] and not s["final"]:
                        times_gain(t)
                if s["final"]:
                    wait_gain(q)
                    rsqrt_chain(stat, FINAL_NORM, FINAL_NORM + NT, chain, D)
                    chain += 1
                    xs += NT
                    for t in range(NT):
                        nc.vector.scalar_tensor_tensor(out=x[:, t, :], in0=x[:, t, :], scalar=stat[:, RS, FINAL_NORM + t:FINAL_NORM + t + 1],
                                                       in1=gain[:, q % 2, :], op0=ALU.mult, op1=ALU.mult).then_inc(x_ready, 1)
                        times_gain(t)
                    dve.sem_inc(gain_used, 1)
                if s["turn"]:
                    for t in range(NT):
                        turned_lo(s, t)
                    dve.sem_inc(gain_used, 1)
                    rsqrt_chain(stat, ROW_NORM, ROW_NORM + NT, chain, D)
                    nc.vector.tensor_scalar(stat[:, NEG_RS, ROW_NORM:ROW_NORM + NT], stat[:, RS, ROW_NORM:ROW_NORM + NT], -1.0, None,
                                            ALU.mult).then_inc(norm_ready, 1)

            def ffn(index, s, iters, gated):
                dslots = [2] if gated else [2, 3]
                up0, gt0 = s["n_up"], s["n_gt"]
                kt = 2 if gated else 4

                def hidden_lo(i):
                    dve.wait_ge(hhi_ready, i + (up0 + 1))
                    nc.vector.tensor_tensor(hlo[:, :, 0:kt, :], ps[:, 6:8, 0:kt * P].rearrange("p t (k n) -> p t k n", k=kt),
                                            hhi[:, :, 0:kt, :].bitcast(F32), ALU.subtract).then_inc(hlo_ready, 1)

                def gate(i):
                    if not gated:
                        return
                    dve.wait_ge(sig_ready, i + (gt0 + 1))
                    for t in range(NT):
                        ins = nc.vector.scalar_tensor_tensor(out=R[:, t, 0:FF1_STEP], in0=ps[:, 4 + t, 0:FF1_STEP],
                                                             scalar=stat[:, RS, ROW_NORM + t:ROW_NORM + t + 1], in1=EG[:, t, :],
                                                             op0=ALU.mult, op1=ALU.mult)
                    ins.then_inc(gact_ready, 1)
                    dve.wait_ge(gact_ready, i + (gt0 + 1))
                    for t in range(NT):
                        ins = nc.vector.scalar_tensor_tensor(out=H[:, t, 0:FF1_STEP], in0=ps[:, 4 + t, FF1_STEP:2 * FF1_STEP],
                                                             scalar=stat[:, RS, ROW_NORM + t:ROW_NORM + t + 1],
                                                             in1=R[:, t, 0:FF1_STEP], op0=ALU.mult, op1=ALU.mult)
                    ins.then_inc(h_ready, 1)

                def body(i, n, after):
                    hidden_lo(i - 1)
                    for q in dslots:
                        split_lo(q, n[q])
                    after(0)
                    gate(i)
                    after(1)

                split_next([0])
                gate(0)
                split_next([1])

                def step_of(i, base):
                    body(i, {q: (i - 1) + base[q] for q in dslots}, lambda q: split_lo(q, (i - 1) + base[q]))

                base = list(slots.n)
                step_of(1, base)
                with dve.Fori(2, iters - 1) as i:
                    step_of(i, base)
                for q in [0, 1] + dslots:
                    slots.n[q] += iters - 2
                following = more_weights(index)
                body(iters - 1, {q: slots.take(q) for q in dslots}, lambda q: split_next([q]) if following else None)
                hidden_lo(iters - 1)
                split_next(dslots)

            def lin(index, s):
                n0 = list(slots.n)
                with dve.Fori(0, s["doubles"] - 1) as d:
                    for q in (2, 3, 0, 1):
                        split_lo(q, d + n0[q])
                for q in range(4):
                    slots.n[q] += s["doubles"] - 1
                split_next([2, 3])
                split_early(index)

            def copy_t(base, b, scale=1.0, dst=None):
                dve.wait_ge(qk_tr, base + b + 1)
                d = dst if dst is not None else arena[:, b * BANK:(b + 1) * BANK]
                if scale == 1.0:
                    nc.vector.tensor_copy(d, ps[:, b % 4, :]).then_inc(qk_dve, 1)
                else:
                    nc.vector.tensor_scalar(d, ps[:, b % 4, :], scale, None, ALU.mult).then_inc(qk_dve, 1)

            def mixed_lo(s, b):
                dve.wait_ge(xhi_ready, 4 * s["n_xt"] + b + 1)
                nc.vector.tensor_tensor(xlo[:, 2 * b:2 * b + 2, :], ps[:, b, :].rearrange("p (k n) -> p k n", k=2),
                                        xhi[:, 2 * b:2 * b + 2, :].bitcast(F32), ALU.subtract).then_inc(xlo_ready, 1)

            def mix_ab(s):
                dve.wait_ge(bias_sem, 16)
                step(nc.vector.memset(BIAS[0:64, :, 0:64], FAR))
                dve.wait_ge(lin_evac, s["n_lin"] - 10 + 3)
                step(nc.vector.tensor_scalar(wsc[:], proj[:, :, C_WI:C_WI + 8], 8.0 ** -0.5, None, ALU.mult))
                for b in range(1, 9, 2):
                    copy_t(0, b)
                for h in range(8):
                    dve.wait_ge(ix_relu, h + 1)
                    for t, (a, b) in enumerate(((256, 384), (0, 256))):
                        if h == 0:
                            ins = nc.vector.tensor_scalar(IXS[:, a:b], REL[0][:, a:b], wsc[:, t, 0:1], None, ALU.mult)
                        else:
                            ins = nc.vector.scalar_tensor_tensor(out=IXS[:, a:b], in0=REL[h % 2][:, a:b],
                                                                 scalar=wsc[:, t, h:h + 1], in1=IXS[:, a:b],
                                                                 op0=ALU.mult, op1=ALU.add)
                        if t == 0:
                            ins.then_inc(dve_step, 1)
                            step.n += 1
                    ins.then_inc(ix_acc, 1)
                    dve.wait_ge(dve_step, step.n)
                    dve.wait_ge(ix_acc, h + 1)
                step(nc.vector.memset(IXS[0:64, 192:256], FAR))
                step(nc.vector.memset(IXS[0:64, 320:384], FAR))

                def top_round():
                    for t, (a, b) in enumerate(((256, 384), (0, 256))):
                        nc.vector.max(top8[:, t, :], IXS[:, a:b]).then_inc(dve_step, 1)
                        step.n += 1
                    for t, (a, b) in enumerate(((256, 384), (0, 256))):
                        dve.wait_ge(dve_step, step.n - 1 if t == 0 else step.n - 1)
                        nc.vector.match_replace(IXS[:, a:b], top8[:, t, :], IXS[:, a:b], TAKEN).then_inc(dve_step, 1)
                        step.n += 1

                def negated(u):
                    dve.wait_ge(score_ready, u + 1)
                    if u >= 4:
                        dve.wait_ge(ptr_ready, u - 3)
                    bank = ps[:, 4 + u % 2, :]
                    if u < 8:
                        nc.vector.scalar_tensor_tensor(out=SC[u % 4][:, 0:256], in0=bank[:, 0:256], scalar=-0.125,
                                                       in1=BIAS[:, u, 255::-1], op0=ALU.mult, op1=ALU.subtract)
                        nc.vector.scalar_tensor_tensor(out=SC[u % 4][:, 256:384], in0=bank[:, 256:384], scalar=-0.125,
                                                       in1=BIAS[:, u, 127::-1], op0=ALU.mult, op1=ALU.subtract
                                                       ).then_inc(biased, 1)
                    else:
                        nc.vector.scalar_tensor_tensor(out=SC[u % 4], in0=bank[:, 0:SPAN], scalar=-0.125, in1=MSK,
                                                       op0=ALU.mult, op1=ALU.subtract).then_inc(biased, 1)

                def least(u):
                    dve.wait_ge(biased, u + 1)
                    nc.vector.tensor_reduce(unit_stat[:, 0, u % 4, 0:1], SC[u % 4][:, 256:384], AX_X, ALU.min)
                    nc.vector.tensor_reduce(unit_stat[:, 0, u % 4, 1:2], SC[u % 4][:, 0:256], AX_X, ALU.min
                                            ).then_inc(nmax_ready, 1)

                for u in range(19):
                    if u == 8:
                        dve.wait_ge(dve_step, step.n)
                        step(nc.vector.tensor_scalar(MSK, IXS, TAKEN, 1.0, ALU.is_equal, ALU.subtract))
                        step(nc.vector.tensor_scalar(MSK, MSK, -FAR, None, ALU.mult))
                    if u < 16:
                        negated(u)
                    if 1 <= u < 17:
                        dve.wait_ge(p_exp, u)
                        nc.vector.reciprocal(unit_stat[:, 2, (u - 1) % 4, :], unit_stat[:, 1, (u - 1) % 4, :]
                                             ).then_inc(rden_ready, 1)
                    if u < 16:
                        least(u)
                    if u < TOPK // 8:
                        dve.wait_ge(dve_step, step.n)
                        top_round()
                    if u >= 3 and (u - 3) % 4 == 3 and u < 18:
                        mixed_lo(s, (u - 3) // 4)
                mixed_lo(s, 3)

            def branch(s):
                sa, sbr = proj[:, :, C_GA:C_GA + D], proj[:, :, C_GB:C_GB + D]
                dve.wait_ge(branch_gates, 1)
                dve.wait_ge(br_ready, 1)
                for t in range(NT):
                    step(nc.vector.tensor_tensor(Y[:, t, :], acc_tile(t), sa[:, t, :], ALU.mult))
                dve.wait_ge(branch_gates, 2)
                dve.wait_ge(br_ready, 2)
                for t in range(NT):
                    pb = ps[:, 4 + 2 * t:6 + 2 * t, :].rearrange("p b n -> p (b n)")
                    step(nc.vector.tensor_tensor(sbr[:, t, :], pb, sbr[:, t, :], ALU.mult))
                    nc.vector.tensor_tensor(Y[:, t, :], Y[:, t, :], sbr[:, t, :], ALU.add).then_inc(y_ready, 1)

            def mix_sb(s):
                base = s["n_qk"]
                for b in range(1, 8, 2):
                    copy_t(base, b, scale=0.125 if b < 4 else 1.0)
                u0 = 16 * s["n_sb"]
                for u in range(18):
                    if u < 16:
                        dve.wait_ge(l_ready, u0 + u + 1)
                        if u >= 4:
                            dve.wait_ge(suf_ready, u0 + u - 3)
                        z = ps[:, 4 + u % 2, 0:SPAN]
                        nc.vector.scalar_tensor_tensor(out=SN[u % 4], in0=z, scalar=0.0, in1=SA[u % 4],
                                                       op0=ALU.max, op1=ALU.add).then_inc(sp_ready, 1)
                        nc.vector.scalar_tensor_tensor(out=SL[u % 4], in0=z, scalar=0.0, in1=SA[u % 4],
                                                       op0=ALU.min, op1=ALU.subtract).then_inc(lb_ready, 1)
                    v = u - 1
                    if 0 <= v < 16:
                        dve.wait_ge(suf_ready, u0 + v + 1)
                        dve.wait_ge(lb_ready, u0 + v + 1)
                        if v >= 4:
                            dve.wait_ge(sbpv_ready, u0 + v - 3)
                        nc.vector.tensor_tensor(SW[v % 4], SL[v % 4], ps[:, 6 + v % 2, 0:SPAN], ALU.subtract
                                                ).then_inc(arg_ready, 1)
                    if v >= 3 and (v - 3) % 4 == 3 and u < 18:
                        mixed_lo(s, (v - 3) // 4 - 0) if (v - 3) // 4 < 3 else None
                mixed_lo(s, 3)

            def mix_conv(s):
                base = s["n_qk"]
                dve.wait_ge(lin_evac, s["n_lin"])
                nc.vector.tensor_tensor(proj[:, 0, D:2 * D], proj[:, 0, D:2 * D], proj[:, 0, 2 * D:3 * D], ALU.mult
                                        ).then_inc(cu_dve, 1)
                step(nc.vector.memset(HT[:, :, 0:2], 0.0))
                for b in range(1, 8, 2):
                    if b < 4:
                        copy_t(base, b, dst=BT[:, 2 * b:2 * b + 2, :].rearrange("p k n -> p (k n)"))
                    else:
                        dve.wait_ge(qk_tr, base + b + 1)
                        nc.vector.tensor_copy(HT[:, 2 * b - 8:2 * b - 6, 2:258],
                                              ps[:, b % 4, :].rearrange("p (k n) -> p k n", k=2)).then_inc(qk_dve, 1)
                dve.wait_ge(qk_act, s["n_qka"] + 4)
                for k in range(KT):
                    dve.wait_ge(tap0_ready, k + 1)
                    for j in (1, 2):
                        step(nc.vector.scalar_tensor_tensor(out=AC[:, k, :], in0=HT[:, k, j:j + 256], scalar=cw[:, k, j:j + 1],
                                                            in1=AC[:, k, :], op0=ALU.mult, op1=ALU.add))
                    nc.vector.tensor_tensor(AC[:, k, :], AC[:, k, :], BT[:, k, :], ALU.mult).then_inc(conv_ready, 1)
                for b in range(4):
                    dve.wait_ge(xhi_ready, 4 * s["n_xt"] + b + 1)
                    nc.vector.tensor_tensor(xlo[:, 2 * b:2 * b + 2, :], AC[:, 2 * b:2 * b + 2, :],
                                            xhi[:, 2 * b:2 * b + 2, :].bitcast(F32), ALU.subtract).then_inc(xlo_ready, 1)

            def mix_gla(s):
                base = s["n_qk"]
                for b in range(1, 4, 2):
                    copy_t(base, b, scale=128.0 ** -0.5 if b < 2 else 1.0, dst=GQK[:, b * BANK:(b + 1) * BANK])
                for j in range(4):
                    dve.wait_ge(gate_ps, j // 2 + 1)
                    ins = nc.vector.tensor_scalar(GC[:, j * 256:(j + 1) * 256], ps[:, 5 + j // 2, (j % 2) * 256:(j % 2 + 1) * 256],
                                                  bgate[:, j:j + 1], None, ALU.add)
                    if j < 3:
                        step(ins)
                ins.then_inc(gz_ready, 1)
                dve.wait_ge(gz_ready, 1)
                step(nc.vector.memset(GQX, 1.0))
                step(nc.vector.memset(GQX.rearrange("p (c n) -> p c n", n=64)[:, :, 0:1], 0.0))
                dve.wait_ge(gl_ready, 1)
                step(nc.vector.scalar_tensor_tensor(out=GC, in0=GC, scalar=0.0, in1=GL, op0=ALU.min, op1=ALU.subtract))
                step(nc.vector.tensor_tensor_scan(GL, GQX, GC, 0.0, ALU.mult, ALU.add))
                nc.vector.tensor_scalar(GC, GL, 1.0 / 16.0, None, ALU.mult).then_inc(cum_ready, 1)
                dve.wait_ge(cum_ready, 1)
                c16 = GC.rearrange("p (b n) -> p b n", n=16)
                c64 = GC.rearrange("p (c n) -> p c n", n=64)
                nc.vector.tensor_tensor(GQX.rearrange("p (b n) -> p b n", n=16), c16, c16[:, :, 7:8].to_broadcast([P, 64, 16]),
                                        ALU.subtract).then_inc(gdiff_ready, 1)
                for a in range(4):
                    w = 16 * (a + 1)
                    nc.vector.tensor_tensor(GK[a].rearrange("p (c n) -> p c n", n=w),
                                            c64[:, :, 16 * a + 7:16 * a + 8].to_broadcast([P, 16, w]), c64[:, :, 0:w],
                                            ALU.subtract).then_inc(gdiff_ready, 1)
                nc.vector.tensor_tensor(GKS.rearrange("p (c n) -> p c n", n=64), c64[:, :, 63:64].to_broadcast([P, 16, 64]), c64,
                                        ALU.subtract).then_inc(gdiff_ready, 1)
                nc.vector.tensor_copy(EL.rearrange("p (c n) -> p c n", n=1), c64[:, :, 63:64]).then_inc(gdiff_ready, 1)
                dve.wait_ge(qk_act, s["n_qka"] + 2)
                dve.wait_ge(gx_ready, 2)
                nc.vector.tensor_tensor(GQX, GQX, GQK[:, 0:1024], ALU.mult).then_inc(qk_scaled, 1)
                kt64 = GQK[:, 1024:2048].rearrange("p (c n) -> p c n", n=64)
                for a in range(4):
                    w = 16 * (a + 1)
                    dve.wait_ge(gx_ready, 3 + a)
                    g = GK[a].rearrange("p (c n) -> p c n", n=w)
                    nc.vector.tensor_tensor(g, g, kt64[:, :, 0:w], ALU.mult).then_inc(qk_scaled, 1)
                step(nc.vector.memset(GS, 0.0))
                dve.wait_ge(gs_ready, 1)
                for half in (0, 64):
                    for a in range(4):
                        w = 16 * (a + 1)
                        o = GS[half:half + w, :].rearrange("p (g n) -> p g n", n=64)[:, :, 16 * a:16 * a + 16]
                        i0 = ps[half:half + w, 4, :].rearrange("p (g n) -> p g n", n=64)[:, :, 16 * a:16 * a + 16]
                        m = const[half:half + w, K_LE + 16 * a:K_LE + 16 * a + 16].unsqueeze(1).to_broadcast([w, 8, 16])
                        ins = nc.vector.tensor_tensor(o, i0, m, ALU.mult)
                        if not (half == 64 and a == 3):
                            step(ins)
                ins.then_inc(gs_sb, 1)
                dve.wait_ge(swish_ready, 1)
                e = proj[:, :, 0:D]
                step(nc.vector.tensor_tensor(e, e, proj[:, :, 2 * D:3 * D], ALU.mult))
                for n in range(3):
                    dve.wait_ge(upd_ready, n + 1)
                    if n == 0:
                        nc.vector.tensor_copy(GST, ps[:, 6:8, :].rearrange("p b n -> p (b n)")).then_inc(state_ready, 1)
                    else:
                        dve.wait_ge(gx_ready, 8)
                        for h in range(4):
                            ins = nc.vector.scalar_tensor_tensor(
                                out=GST[:, h * 256:(h + 1) * 256], in0=GST[:, h * 256:(h + 1) * 256],
                                scalar=EL[:, 4 * h + n:4 * h + n + 1],
                                in1=ps[:, 6 + h // 2, (h % 2) * 256:(h % 2 + 1) * 256], op0=ALU.mult, op1=ALU.add)
                            if h < 3:
                                step(ins)
                        ins.then_inc(state_ready, 1)
                    dve.wait_ge(state_ready, n + 1)
                rsqrt_chain(gstat, 0, 8, s["n_chain"], 256)
                q = s["n_gain"]
                wait_gain(q)
                for t in range(NT):
                    for h in range(4):
                        ins = nc.vector.scalar_tensor_tensor(
                            out=Y[:, t, h * 256:(h + 1) * 256], in0=acc_tile(t)[:, h * 256:(h + 1) * 256],
                            scalar=gstat[:, RS, 4 * t + h:4 * t + h + 1], in1=gain[:, q % 2, h * 256:(h + 1) * 256],
                            op0=ALU.mult, op1=ALU.mult)
                        if not (t == 1 and h == 3):
                            step(ins)
                ins.then_inc(gain_used, 1)
                dve.wait_ge(gain_used, q + 1)
                for t in range(NT):
                    nc.vector.tensor_tensor(Y[:, t, :], Y[:, t, :], e[:, t, :], ALU.mult).then_inc(y_ready, 1)

            split_early(-1)
            for index, s in enumerate(STAGES):
                kind = s["kind"]
                if kind == "bound":
                    bound(s)
                elif kind == "turn":
                    for t in range(NT):
                        turned_lo(s, t)
                elif kind == "gated":
                    ffn(index, s, FF1_ITERS, True)
                elif kind == "squared":
                    ffn(index, s, FF2_ITERS, False)
                elif kind == "lin":
                    lin(index, s)
                elif kind in ("out", "branch"):
                    split_next([2, 3])
                    split_early(index)
                    if kind == "branch":
                        branch(s)
                elif kind == "mix_ab":
                    mix_ab(s)
                elif kind == "mix_sb":
                    mix_sb(s)
                elif kind == "mix_conv":
                    mix_conv(s)
                elif kind == "mix_gla":
                    mix_gla(s)

        @block.gpsimd
        def _(pool):
            step = Steps(pool, pool_step)
            line = bass.AP(tensor=bias_line.tensor, offset=0, ap=[[1, P], [383, 8], [1, 256]])
            pool.wait_ge(const_sem, 16)
            pool.wait_ge(x_tile_in[1], 16)
            pool.wait_ge(raw_in[1], 16)
            pool.dma_start(BIAS, line).then_inc(bias_sem, 16)

            def squared(s):
                up0 = s["n_up"]

                def square(i):
                    pool.wait_ge(relu_ready, i + (s["n_sq"] + 1))
                    if not isinstance(i, int) or i >= 1:
                        pool.wait_ge(ht_ready, i + up0)
                    nc.gpsimd.tensor_tensor(H[:], R[:], R[:], ALU.mult).then_inc(h_ready, 1)

                square(0)
                with pool.Fori(1, FF2_ITERS) as i:
                    square(i)

            def mix_ab(s):
                pool.wait_ge(lin_evac, s["n_lin"] - 10 + 3)
                for t in range(NT):
                    v = proj[:, t, 0:ROPE_HEADS * 64].rearrange("p (h e) -> p h e", e=64)
                    cos = const[:, K_COS + 16 * t:K_COS + 16 * t + 16].unsqueeze(1).to_broadcast([P, ROPE_HEADS, 16])
                    step(nc.gpsimd.tensor_tensor(ROPE_A, v[:, :, 0:16], cos, ALU.mult))
                    for half in (0, 8):
                        sin = const[:, K_SIN + 16 * t + half:K_SIN + 16 * t + half + 8].unsqueeze(1).to_broadcast([P, ROPE_HEADS, 8])
                        step(nc.gpsimd.tensor_tensor(ROPE_B[:, :, half:half + 8], v[:, :, 8 - half:16 - half], sin, ALU.mult))
                    nc.gpsimd.tensor_tensor(v[:, :, 0:16], ROPE_A, ROPE_B, ALU.add).then_inc(rope_done, 1)
                    pool.wait_ge(rope_done, t + 1)
                for u in range(16):
                    pool.wait_ge(rden_ready, u + 1)
                    for t, (a, b) in enumerate(((256, 384), (0, 256))):
                        nc.gpsimd.tensor_scalar(SC[u % 4][:, a:b], SC[u % 4][:, a:b], unit_stat[:, 2, u % 4, t:t + 1], None,
                                                ALU.mult).then_inc(p_ready, 1)

            def mix_sb(s):
                u0 = 16 * s["n_sb"]
                causal = const[:, K_LT:K_LT + P].unsqueeze(1).to_broadcast([P, 2, P])

                def diagonal(buf):
                    return buf.rearrange("p (b n) -> p b n", n=P)[:, 0:3:2, :]

                for u in range(18):
                    if u < 16:
                        pool.wait_ge(sp_ready, u0 + u + 1)
                        nc.gpsimd.tensor_tensor(diagonal(SN[u % 4]), diagonal(SN[u % 4]), causal, ALU.mult).then_inc(spm_ready, 1)
                    v = u - 2
                    if v >= 0:
                        pool.wait_ge(w_exp, u0 + v + 1)
                        nc.gpsimd.tensor_tensor(diagonal(SW[v % 4]), diagonal(SW[v % 4]), causal, ALU.mult).then_inc(w_ready, 1)

            def mix_gla(s):
                pool.wait_ge(qk_act, s["n_qka"] + 2)
                pool.wait_ge(qk_dve, s["n_qkd"] + 2)
                pool.wait_ge(gx_ready, 1)
                nc.gpsimd.tensor_tensor(GQI, GQI, GQK[:, 0:1024], ALU.mult).then_inc(qk_pool, 1)
                pool.wait_ge(gx_ready, 7)
                nc.gpsimd.tensor_tensor(GKS, GKS, GQK[:, 1024:2048], ALU.mult).then_inc(qk_pool, 1)

            for s in STAGES:
                kind = s["kind"]
                if kind == "squared":
                    squared(s)
                elif kind == "mix_ab":
                    mix_ab(s)
                elif kind == "mix_sb":
                    mix_sb(s)
                elif kind == "mix_conv":
                    pool.wait_ge(lin_evac, s["n_lin"])
                    nc.gpsimd.tensor_tensor(proj[:, 1, D:2 * D], proj[:, 1, D:2 * D], proj[:, 1, 2 * D:3 * D], ALU.mult
                                            ).then_inc(cu_pool, 1)
                elif kind == "mix_gla":
                    mix_gla(s)

        @block.tensor
        def _(pe):
            slots = Slots()
            pe.wait_ge(const_sem, 16)

            def split_mm(out_ap, a_hi, a_lo, w_slot, panel, first, last):
                wh = whi[w_slot][:, panel * BANK:(panel + 1) * BANK]
                wl = wlo[w_slot][:, panel * BANK:(panel + 1) * BANK]
                nc.tensor.matmul(out_ap, a_hi, wh, start=first, stop=False)
                nc.tensor.matmul(out_ap, a_hi, wl, start=False, stop=False)
                return nc.tensor.matmul(out_ap, a_lo, wh, start=False, stop=last)

            def job(banks, slot_ids, n, last_sem=None):
                for j, s in enumerate(slot_ids):
                    pe.wait_ge(lo_ready[s], n[s] + 1)
                    for kk in range(PANELS):
                        k = j * PANELS + kk
                        for t in range(NT):
                            ins = split_mm(ps[:, banks[t], :], xhi[:, k, t * P:(t + 1) * P], xlo[:, k, t * P:(t + 1) * P],
                                           s, kk, k == 0, k == KT - 1)
                    ins.then_inc(w_used[s] if j == 0 or last_sem is None else last_sem, 1)

            def job_by_tile(s, banks, slot_ids, n, acc=False):
                turn = s.get("turns_here") if slot_ids[0] == 0 else None
                for t in range(NT):
                    if turn is not None and t == 0:
                        turn_y(turn, 0)
                    pe.wait_ge(xlo_ready, 4 * (s["n_xt"] - 1) + (2 + 2 * t if turn is not None else 4))
                    for j, q in enumerate(slot_ids):
                        if t == 0:
                            pe.wait_ge(lo_ready[q], n[q] + 1)
                        for kk in range(PANELS):
                            k = j * PANELS + kk
                            ins = split_mm(ps[:, banks[t], :], xhi[:, k, t * P:(t + 1) * P], xlo[:, k, t * P:(t + 1) * P],
                                           q, kk, k == 0, k == KT - 1)
                        if turn is not None and t == 0 and j == 0:
                            turn_y(turn, 1)
                        if t == NT - 1 and not (acc and j == 1):
                            ins.then_inc(w_used[q], 1)
                    if acc:
                        ins.then_inc(acc_ready, 1)
                if acc:
                    pe.wait_ge(acc_ready, NT * (s["n_acc"] + 1))
                    pe.sem_inc(w_used[slot_ids[1]], 1)

            def wide(slot_ids, n, a_hi, a_lo, kt, first, last, bank0=0, last_sem=None):
                for j, s in enumerate(slot_ids):
                    pe.wait_ge(lo_ready[s], n[s] + 1)
                    for kk in range(2):
                        k = 2 * j + kk
                        for t in range(NT):
                            for c in range(2):
                                ins = split_mm(ps[:, bank0 + 2 * t + c, :], a_hi(t, k), a_lo(t, k), s, 2 * kk + c,
                                               first and k == 0, last and k == kt - 1)
                    ins.then_inc(w_used[s] if j + 1 < len(slot_ids) or last_sem is None else last_sem, 1)

            def ffn(s, iters, gated):
                dslots = [2] if gated else [2, 3]
                up0 = s["n_up"]
                kt = 2 if gated else 4

                def up(n):
                    job((4, 5), (0, 1), n)

                def down(i, n, first):
                    pe.wait_ge(hlo_ready, i + (up0 + 1))
                    wide(dslots, n, lambda t, k: hhi[:, t, k, :], lambda t, k: hlo[:, t, k, :], kt, first, False)

                def turn(i):
                    pe.wait_ge(h_ready, i + (up0 + 1))
                    for t in range(NT):
                        for k in range(kt):
                            ins = nc.tensor.transpose(ps[:, 6 + t, k * P:(k + 1) * P], H[:, t, k * P:(k + 1) * P], ident)
                    ins.then_inc(ht_ready, 1)

                ids = [0, 1] + dslots
                job_by_tile(s, (4, 5), (0, 1), {q: slots.take(q) for q in (0, 1)})
                turn(0)
                n = {q: slots.take(q) for q in ids}
                up(n)
                down(0, n, True)
                turn(1)
                base = list(slots.n)
                with pe.Fori(2, iters) as i:
                    n = {q: (i - 2) + base[q] for q in ids}
                    up(n)
                    down(i - 1, n, False)
                    turn(i)
                for q in ids:
                    slots.n[q] += iters - 2
                n = {q: slots.take(q) for q in dslots}
                pe.wait_ge(hlo_ready, up0 + iters)
                for t in range(NT):
                    for j, q in enumerate(dslots):
                        if t == 0:
                            pe.wait_ge(lo_ready[q], n[q] + 1)
                        for kk in range(2):
                            k = 2 * j + kk
                            for c in range(2):
                                ins = split_mm(ps[:, 2 * t + c, :], hhi[:, t, k, :], hlo[:, t, k, :], q, 2 * kk + c,
                                               False, k == kt - 1)
                        if t == NT - 1 and j + 1 < len(dslots):
                            ins.then_inc(w_used[q], 1)
                    ins.then_inc(acc_ready, 1)
                pe.wait_ge(acc_ready, NT * (s["n_acc"] + 1))
                pe.sem_inc(w_used[dslots[-1]], 1)

            def lin(s):
                base = s["n_lin"]

                def two(d, n, first):
                    for c in range(2):
                        if not first:
                            pe.wait_ge(lin_evac, d * 2 + (base + c - 1))
                        ids = (0, 1) if c == 0 else (2, 3)
                        if first and c == 0:
                            job_by_tile(s, (4, 5), ids, n)
                        else:
                            job((4 + 2 * c, 5 + 2 * c), ids, n)

                two(0, {q: slots.take(q) for q in range(4)}, True)
                n0 = list(slots.n)
                with pe.Fori(1, s["doubles"]) as d:
                    two(d, {q: (d - 1) + n0[q] for q in range(4)}, False)
                for q in range(4):
                    slots.n[q] += s["doubles"] - 1

            def out_layer(s):
                job_by_tile(s, (0, 2), (0, 1), {q: slots.take(q) for q in (0, 1)})
                job_by_tile(s, (1, 3), (2, 3), {q: slots.take(q) for q in (2, 3)}, acc=True)

            def branch(s):
                pe.wait_ge(xlo_ready, 4 * s["n_xt"])
                for c in range(2):
                    ids = (0, 1) if c == 0 else (2, 3)
                    n = {q: slots.take(q) for q in ids}
                    wide(ids, n, lambda t, k: xhi[:, 4 * c + k, t * P:(t + 1) * P],
                         lambda t, k: xlo[:, 4 * c + k, t * P:(t + 1) * P], 4, True, True, bank0=4 * c, last_sem=br_ready)
                    pe.wait_ge(br_ready, c + 1)
                    pe.sem_inc(w_used[ids[1]], 1)

            def turn_y(s, t):
                pe.wait_ge(y_ready, NT * s["y"] + t + 1)
                for half in range(2):
                    for k in range(4):
                        f = (4 * half + k) * P
                        ins = nc.tensor.transpose(ps[:, 2 * t + half, k * P:(k + 1) * P], Y[:, t, f:f + P], ident)
                    ins.then_inc(tr_ready, 1)

            def turn_tiles(s, columns, before=None):
                for b in range(len(columns) // 2):
                    if before is not None:
                        before(b)
                    if b >= 4:
                        if b % 2 == 0:
                            pe.wait_ge(qk_act, s["n_qka"] + (b - 4) // 2 + 1)
                        else:
                            pe.wait_ge(qk_dve, s["n_qkd"] + (b - 4) // 2 + 1)
                    for j in range(2):
                        for t in range(NT):
                            c = columns[2 * b + j]
                            ins = nc.tensor.transpose(ps[:, b % 4, j * 256 + t * P:j * 256 + (t + 1) * P],
                                                      proj[:, t, c:c + P], ident)
                    ins.then_inc(qk_tr, 1)
                nb = len(columns) // 2
                return nb

            def wait_tiles(s, nb):
                pe.wait_ge(qk_act, s["n_qka"] + (nb + 1) // 2)
                pe.wait_ge(qk_dve, s["n_qkd"] + nb // 2)

            def tile_of(i):
                return arena[:, i * 256:(i + 1) * 256]

            def mix_ab(s):
                jobs0 = s["n_lin"] - 10
                columns = [P * j for j in range(10)] + [C_QA + P * j for j in range(8)]

                def before(b):
                    if b == 0:
                        pe.wait_ge(rope_done, NT)
                    if b == 5:
                        pe.wait_ge(lin_evac, jobs0 + 5)

                nb = turn_tiles(s, columns, before)
                wait_tiles(s, nb)

                def scores(bank, q, k, r):
                    qt, kt = tile_of(q)[64 * r:64 * r + 64, :], tile_of(k)[64 * r:64 * r + 64, :]
                    nc.tensor.matmul(ps[:, bank, 0:256], qt[:, P:2 * P], kt, start=True, stop=True)
                    return nc.tensor.matmul(ps[:, bank, 256:384], qt[:, 0:P], kt[:, 0:P], start=True, stop=True)

                pe.wait_ge(lin_evac, s["n_lin"])
                for h in range(8):
                    if h >= 4:
                        pe.wait_ge(ix_relu, h - 3)
                    scores(4 + h % 4, 4 + h // 2, 9, h % 2).then_inc(ix_ready, 1)
                pe.wait_ge(ix_relu, 8)
                for u in range(19):
                    if u < 16:
                        if u >= 2:
                            pe.wait_ge(biased, u - 1)
                        if u < 8:
                            ins = scores(4 + u % 2, 10 + u // 2, 14 + u // 2, u % 2)
                        else:
                            ins = scores(4 + u % 2, (u - 8) // 2, 8, u % 2)
                        ins.then_inc(score_ready, 1)
                    v = u - 2
                    if 0 <= v < 16:
                        pe.wait_ge(p_ready, 2 * v + 2)
                        if v >= 2:
                            pe.wait_ge(pt_ready, v - 1)
                        bank = 6 + v % 2
                        nc.tensor.transpose(ps[:, bank, 0:128], SC[v % 4][:, 256:384], ident)
                        nc.tensor.transpose(ps[:, bank, 128:256], SC[v % 4][:, 0:128], ident)
                        nc.tensor.transpose(ps[:, bank, 256:384], SC[v % 4][:, 128:256], ident).then_inc(ptr_ready, 1)
                    v = u - 3
                    if v >= 0:
                        pe.wait_ge(pt_ready, v + 1)
                        c = C_VA + 64 * v if v < 8 else C_VB + 64 * (v % 2)
                        pair, r = v // 2, v % 2
                        o = ps[64 * r:64 * r + 64, pair // 2, (pair % 2) * 256:(pair % 2 + 1) * 256]
                        nc.tensor.matmul(o, proj[:, 0, c:c + 64], PTB[v % 4][:, 0:256], start=True, stop=False)
                        nc.tensor.matmul(o[:, 128:256], proj[:, 1, c:c + 64], PTB[v % 4][:, 256:384], start=False, stop=True
                                         ).then_inc(pv_ready, 1)

            def mix_sb(s):
                u0 = 16 * s["n_sb"]
                pe.wait_ge(lin_evac, s["n_lin"])
                nb = turn_tiles(s, [P * j for j in range(16)])
                wait_tiles(s, nb)
                gt, ones = const[:, K_GT:K_GT + P], const[:, K_ONES:K_ONES + P]
                for u in range(20):
                    if u < 16:
                        if u >= 2:
                            pe.wait_ge(lb_ready, u0 + u - 1)
                        r = u % 2
                        q, k = tile_of(u // 2)[64 * r:64 * r + 64, :], tile_of(8 + u // 2)[64 * r:64 * r + 64, :]
                        nc.tensor.matmul(ps[:, 4 + u % 2, 0:256], k[:, 0:P], q, start=True, stop=True)
                        nc.tensor.matmul(ps[:, 4 + u % 2, 256:384], k[:, P:2 * P], q[:, P:2 * P], start=True, stop=True
                                         ).then_inc(z_ready, 1)
                    v = u - 2
                    if 0 <= v < 16:
                        pe.wait_ge(spm_ready, u0 + v + 1)
                        if v >= 2:
                            pe.wait_ge(arg_ready, u0 + v - 1)
                        bank, n1 = ps[:, 6 + v % 2, :], SN[v % 4]
                        nc.tensor.matmul(bank[:, 256:384], gt, n1[:, 256:384], start=True, stop=True)
                        nc.tensor.matmul(bank[:, 0:256], gt, n1[:, 0:256], start=True, stop=False)
                        nc.tensor.matmul(bank[:, 128:256], ones, n1[:, 256:384], start=False, stop=True).then_inc(suf_ready, 1)
                    v = u - 4
                    if v >= 0:
                        pe.wait_ge(w_ready, u0 + v + 1)
                        pair, r = v // 2, v % 2
                        c = 2 * D + 64 * v
                        o = ps[64 * r:64 * r + 64, pair // 2, (pair % 2) * 256:(pair % 2 + 1) * 256]
                        nc.tensor.matmul(o, proj[:, 0, c:c + 64], SW[v % 4][:, 0:256], start=True, stop=False)
                        nc.tensor.matmul(o[:, 128:256], proj[:, 1, c:c + 64], SW[v % 4][:, 256:384], start=False, stop=True
                                         ).then_inc(sbpv_ready, 1)

            def mix_conv(s):
                pe.wait_ge(lin_evac, s["n_lin"])

                def before(b):
                    if b == 4:
                        pe.wait_ge(cu_dve, 1)
                        pe.wait_ge(cu_pool, 1)

                turn_tiles(s, [P * j for j in range(16)], before)

            def mix_gla(s):
                pe.wait_ge(lin_evac, s["n_lin"])
                pe.wait_ge(small_sem, 64)
                for t in range(NT):
                    o = ps[:, 4, 16 * t:16 * t + 16]
                    for k in range(KT):
                        nc.tensor.matmul(o, xhi[:, k, t * P:(t + 1) * P].bitcast(F32), wlow[:, k, :], start=(k == 0), stop=False)
                        ins = nc.tensor.matmul(o, xlo[:, k, t * P:(t + 1) * P].bitcast(F32), wlow[:, k, :], start=False,
                                               stop=(k == KT - 1))
                ins.then_inc(low_ready, 1)
                turn_tiles(s, [P * j for j in range(8)])
                pe.wait_ge(low_sb, 1)
                for t in range(NT):
                    ins = nc.tensor.transpose(ps[0:16, 7, t * P:(t + 1) * P], LOWN[:, 16 * t:16 * t + 16], ident)
                ins.then_inc(low_ready, 1)
                pe.wait_ge(low_sb, 2)
                for j in range(4):
                    ins = nc.tensor.matmul(ps[:, 5 + j // 2, (j % 2) * 256:(j % 2 + 1) * 256], wup[:, j * P:(j + 1) * P],
                                           LOW[0:16, :], start=True, stop=True)
                    if j % 2 == 1:
                        ins.then_inc(gate_ps, 1)
                pe.wait_ge(qk_scaled, 5)
                for h in range(4):
                    for n in range(4):
                        for a in range(4):
                            w, c = 16 * (a + 1), 4 * h + n
                            half, col = 64 * (n % 2), (2 * h + n // 2) * 64 + 16 * a
                            ins = nc.tensor.matmul(ps[half:half + w, 4, col:col + 16], GK[a][:, c * w:(c + 1) * w],
                                                   GQX[:, c * 64 + 16 * a:c * 64 + 16 * a + 16], start=True, stop=True)
                ins.then_inc(gs_ready, 1)
                pe.wait_ge(qk_pool, 2)
                for h in range(4):
                    for t in range(NT):
                        i = 2 * h + t
                        ins = nc.tensor.transpose(ps[:, 6 + i // 4, (i % 4) * P:(i % 4 + 1) * P],
                                                  GKS[:, i * P:(i + 1) * P], ident)
                        if i % 4 == 3:
                            ins.then_inc(kn_ps, 1)
                wait_tiles(s, 4)
                pe.wait_ge(gs_sb, 1)
                pe.wait_ge(kn_sb, 2)
                for n in range(4):
                    t, half = n // 2, 64 * (n % 2)
                    if n >= 1:
                        pe.wait_ge(state_ready, n)
                    for h in range(4):
                        o = ps[half:half + 64, 2 * t + h // 2, (h % 2) * 256:(h % 2 + 1) * 256]
                        v = proj[half:half + 64, t, D + h * 256:D + (h + 1) * 256]
                        if n >= 1:
                            nc.tensor.matmul(o, GQI[:, (4 * h + n) * 64:(4 * h + n + 1) * 64], GST[:, h * 256:(h + 1) * 256],
                                             start=True, stop=False)
                        ins = nc.tensor.matmul(o, GS[half:half + 64, (2 * h + t) * 64:(2 * h + t + 1) * 64], v,
                                               start=(n == 0), stop=True)
                    if n < 3:
                        for h in range(4):
                            v = proj[half:half + 64, t, D + h * 256:D + (h + 1) * 256]
                            ins = nc.tensor.matmul(ps[:, 6 + h // 2, (h % 2) * 256:(h % 2 + 1) * 256],
                                                   GKN[half:half + 64, (2 * h + t) * P:(2 * h + t + 1) * P], v,
                                                   start=True, stop=True)
                        ins.then_inc(upd_ready, 1)
                ins.then_inc(go_ready, 1)

            for s in STAGES:
                kind = s["kind"]
                if kind == "gated":
                    ffn(s, FF1_ITERS, True)
                elif kind == "squared":
                    ffn(s, FF2_ITERS, False)
                elif kind == "lin":
                    lin(s)
                elif kind == "out":
                    out_layer(s)
                elif kind == "branch":
                    branch(s)
                elif kind == "mix_ab":
                    mix_ab(s)
                elif kind == "mix_sb":
                    mix_sb(s)
                elif kind == "mix_conv":
                    mix_conv(s)
                elif kind == "mix_gla":
                    mix_gla(s)


def tall(w, cols):
    n = w.shape[1] // cols
    return w.reshape(2, PANELS, P, n, cols).transpose(3, 0, 2, 1, 4).reshape(n * 2, P, PANELS * cols)


def flat(w):
    return w.reshape(w.shape[0] // 256, 2, P, D).transpose(0, 2, 1, 3).reshape(-1, P, 2 * D)


def kernel(x, n1_g, ffn1_w_in, ffn1_w_out, n2_g, w_in, rel_bias, w_branch_a, w_branch_b, w_out, n3_g,
           ffn2_w_in, ffn2_w_out, nf_g, norm_gains_2, sb_w_qkv_2, sb_w_o_2, conv_w_in_2, conv_w_2,
           conv_w_out_2, gla_w_in_2, gla_w_gate_up_2, gla_b_gate_2, gla_head_norm_2, gla_w_o_2,
           ffn_w_up_2, ffn_w_down_2):
    import concourse.bacc as _bacc
    from concourse.bass_utils import run_bass_kernel_spmd as _run

    def up_ahead(u, d):
        both = np.concatenate([u[1:], d[:-1]], 1).reshape(-1, P, PART)
        return np.concatenate([u[0], both, d[-1]], 0)

    def gated_parts(wi, wo):
        gate, up = wi[:, :FF1], wi[:, FF1:]
        both = np.concatenate([gate.reshape(D, FF1_ITERS, 1, FF1_STEP), up.reshape(D, FF1_ITERS, 1, FF1_STEP)], 2)
        u = tall(both.reshape(D, FF1_ITERS * BANK), BANK).reshape(FF1_ITERS, 2, P, PART)
        return up_ahead(u, flat(wo).reshape(FF1_ITERS, 1, P, PART))

    def squared_parts(wi, wo):
        u = tall(wi, BANK).reshape(FF2_ITERS, 2, P, PART)
        return up_ahead(u, flat(wo).reshape(FF2_ITERS, 2, P, PART))

    w = w_in[0]
    qa, ka, va, qb, kb, vb, qi, ki, wi, ga, gb = np.split(
        w, [512, 1024, 1536, 2048, 2176, 2304, 2816, 2880, 2888, 3912], axis=1)
    qb = qb.reshape(D, 2, 4, 64).transpose(0, 2, 1, 3).reshape(D, 512)
    w_mix = np.concatenate([qb, qi, kb, ki, ki, vb, wi, np.zeros((D, C_QA - C_WI - 8), w.dtype),
                            qa, ka, va, ga, gb], axis=1)
    w_b = w_branch_b[0].reshape(2, 4, 64, D).transpose(1, 0, 2, 3).reshape(512, D)

    parts = [gated_parts(ffn1_w_in[0], ffn1_w_out[0]), tall(w_mix, BANK), flat(w_branch_a[0]), flat(w_b),
             tall(w_out[0], BANK), gated_parts(ffn2_w_in[0], ffn2_w_out[0])]
    mixers = [(sb_w_qkv_2[0], sb_w_o_2[0]), (conv_w_in_2[0], conv_w_out_2[0]),
              (gla_w_in_2[0][:, :3072], gla_w_o_2[0]), (sb_w_qkv_2[1], sb_w_o_2[1])]
    gain_list = [n1_g[0], n2_g[0], n3_g[0], nf_g]
    for layer in range(DEPTH2):
        wi_l, wo_l = mixers[layer]
        parts += [tall(wi_l, BANK), tall(wo_l, BANK), squared_parts(ffn_w_up_2[layer], ffn_w_down_2[layer])]
        g = norm_gains_2[layer]
        gain_list += [g[0]] + ([gla_head_norm_2[0].reshape(D)] if layer % 3 == 2 else []) + [g[1], g[2], g[3]]

    rel = rel_bias[0]
    arrays = {
        "x": x[0],
        "w_parts": np.concatenate(parts, 0),
        "gains": np.stack(gain_list),
        "const_in": constants(),
        "bias_line": np.concatenate([rel[:, 1:257], np.repeat(rel[:, 256:257], 127, axis=1)], axis=1),
        "conv_w": conv_w_2[0].reshape(3, KT, P).transpose(2, 1, 0),
        "gla_low": gla_w_in_2[0][:, 3072:].reshape(KT, P, 16).transpose(1, 0, 2),
        "gla_up": gla_w_gate_up_2[0],
        "gla_b": gla_b_gate_2[0].reshape(4, P).transpose(1, 0),
    }
    nc = _bacc.Bacc("TRN2", target_bir_lowering=False, num_devices=1)
    feeds, aps = {}, []
    for name, a in arrays.items():
        a = np.ascontiguousarray(a)
        feeds["in_" + name] = a
        aps.append(nc.dram_tensor("in_" + name, a.shape, mybir.dt.from_np(a.dtype), kind="ExternalInput").ap())
    out = nc.dram_tensor("out_0", (SEQ, D), F32, kind="ExternalOutput").ap()
    build(nc, *aps, out)
    r = _run(nc, [feeds], core_ids=[0])
    return r.results[0]["out_0"].reshape(1, SEQ, D)
```
